# Optimizing a Trainium2 kernel written in Bass

```python
import math
import jax, jax.numpy as jnp
from jax import lax
import numpy as np

D_MODEL = 1024
BATCH = 1
SEQ = 256
DEPTH = 1

N_HEADS = 16
HEAD_DIM = 64
ATTN_W = N_HEADS * HEAD_DIM
Q_BLOCK = 128
LRU_W = D_MODEL
N_LRU_BLOCKS = 16
LRU_BLOCK = LRU_W // N_LRU_BLOCKS
CONV_W = 4
LRU_C = 8.0
N_BRANCHES = 2
IN_COLS = 3 * ATTN_W + N_HEADS + 2 * LRU_W + N_BRANCHES * D_MODEL
SPLITS = (ATTN_W, 2 * ATTN_W, 3 * ATTN_W, 3 * ATTN_W + N_HEADS,
          3 * ATTN_W + N_HEADS + LRU_W, 3 * ATTN_W + N_HEADS + 2 * LRU_W)
N_EXPERTS = 32
TOP_K = 4
D_EXPERT = D_MODEL
SWIGLU_ALPHA = 1.702
SWIGLU_LIMIT = 7.0
EXPERT_BLOCK = 256
RMS_EPS = 1e-6

kernel_name = "hybrid_fox_rglru_moe_block"

def rmsnorm(x, scale):
    xf = x.astype(jnp.float32)
    y = xf * lax.rsqrt(jnp.mean(xf * xf, axis=-1, keepdims=True) + RMS_EPS)
    return (y * scale.astype(jnp.float32)).astype(x.dtype)

def forgetting_attention(q, k, v, log_f):
    S = q.shape[1]
    c = jnp.cumsum(log_f, axis=1).transpose(0, 2, 1)
    scale = HEAD_DIM ** -0.5
    outs = []
    for i in range(S // Q_BLOCK):
        q0, q1 = i * Q_BLOCK, (i + 1) * Q_BLOCK
        s = jnp.einsum('bqhd,bkhd->bhqk', q[:, q0:q1], k[:, :q1]).astype(jnp.float32) * scale
        bias = c[:, :, q0:q1, None] - c[:, :, None, :q1]
        causal = (q0 + jnp.arange(Q_BLOCK))[:, None] >= jnp.arange(q1)[None, :]
        s = jnp.where(causal, s + bias, -jnp.inf)
        p = jax.nn.softmax(s, axis=-1).astype(v.dtype)
        outs.append(jnp.einsum('bhqk,bkhd->bqhd', p, v[:, :q1]))
    return jnp.concatenate(outs, axis=1)

def causal_dwconv(x, w, b):
    S = x.shape[1]
    xp = jnp.pad(x, ((0, 0), (CONV_W - 1, 0), (0, 0)))
    return sum(xp[:, j:j + S] * w[j] for j in range(CONV_W)) + b

def block_diag_linear(xh, w, b):
    return jnp.einsum('bsni,nij->bsnj', xh, w) + b

def rg_lru(x, wa, ba, wx, bx, lam):
    B, S, W = x.shape
    xh = x.reshape(B, S, N_LRU_BLOCKS, LRU_BLOCK)
    r = jax.nn.sigmoid(block_diag_linear(xh, wa, ba)).reshape(B, S, W)
    i = jax.nn.sigmoid(block_diag_linear(xh, wx, bx)).reshape(B, S, W)
    log_a = -LRU_C * r.astype(jnp.float32) * jax.nn.softplus(-lam.astype(jnp.float32))
    a = jnp.exp(log_a)
    mult = jnp.sqrt(-jnp.expm1(2.0 * log_a))
    mult = jnp.where(jnp.arange(S)[None, :, None] == 0, 1.0, mult)
    b = mult * (i * x).astype(jnp.float32)

    def combine(left, right):
        a1, b1 = left
        a2, b2 = right
        return a1 * a2, a2 * b1 + b2

    _, h = lax.associative_scan(combine, (a, b), axis=1)
    return h.astype(x.dtype)

def hybrid_mixer(xn, w_in, f_bias, gate_bias, conv_w, conv_b, rg_wa, rg_ba, rg_wx, rg_bx,
                 rg_lambda, w_attn_proj, w_rec_proj, w_out):
    B, S, _ = xn.shape
    proj = xn @ w_in
    q, k, v, f_logit, x_rec, y_rec, g_logits = jnp.split(proj, SPLITS, axis=-1)
    q = q.reshape(B, S, N_HEADS, HEAD_DIM)
    k = k.reshape(B, S, N_HEADS, HEAD_DIM)
    v = v.reshape(B, S, N_HEADS, HEAD_DIM)
    log_f = jax.nn.log_sigmoid((f_logit + f_bias).astype(jnp.float32))
    attn = forgetting_attention(q, k, v, log_f).reshape(B, S, ATTN_W)
    rec = rg_lru(causal_dwconv(x_rec, conv_w, conv_b), rg_wa, rg_ba, rg_wx, rg_bx, rg_lambda)
    rec = rec * jax.nn.gelu(y_rec)
    g_attn, g_rec = jnp.split(jax.nn.sigmoid(g_logits + gate_bias), N_BRANCHES, axis=-1)
    merged = g_attn * (attn @ w_attn_proj) + g_rec * (rec @ w_rec_proj)
    return merged @ w_out

def clamped_swiglu(h):
    glu, lin = jnp.split(h, 2, axis=-1)
    glu = jnp.minimum(glu, SWIGLU_LIMIT)
    lin = jnp.clip(lin, -SWIGLU_LIMIT, SWIGLU_LIMIT)
    return glu * jax.nn.sigmoid(SWIGLU_ALPHA * glu) * (lin + 1.0)

def moe_ffn(xn, router_w, router_b, w1, b1, w2, b2):
    B, S, D = xn.shape
    T = B * S
    A = T * TOP_K
    xt = xn.reshape(T, D)
    logits = (xt @ router_w + router_b).astype(jnp.float32)
    top_vals, top_idx = lax.top_k(logits, TOP_K)
    gates = jax.nn.softmax(top_vals, axis=-1)
    flat_e = top_idx.reshape(-1)
    flat_tok = jnp.arange(A, dtype=jnp.int32) // TOP_K
    flat_gate = gates.reshape(-1)
    order = jnp.argsort(flat_e)
    se, stok, sgate = flat_e[order], flat_tok[order], flat_gate[order]
    counts = jnp.bincount(flat_e, length=N_EXPERTS)
    padded = (counts + EXPERT_BLOCK - 1) // EXPERT_BLOCK * EXPERT_BLOCK
    pad_end = jnp.cumsum(padded)
    pad_start = pad_end - padded
    start = jnp.cumsum(counts) - counts
    dest = pad_start[se] + jnp.arange(A) - start[se]
    n_blocks = (A + EXPERT_BLOCK - 1) // EXPERT_BLOCK + N_EXPERTS
    P = n_blocks * EXPERT_BLOCK
    row_tok = jnp.full((P,), T, dtype=jnp.int32).at[dest].set(stok)
    row_gate = jnp.zeros((P,), jnp.float32).at[dest].set(sgate)
    block_expert = jnp.minimum(
        jnp.searchsorted(pad_end, jnp.arange(n_blocks) * EXPERT_BLOCK, side='right'), N_EXPERTS - 1)
    x_pad = jnp.concatenate([xt, jnp.zeros((1, D), xt.dtype)], axis=0)

    def step(acc, blk):
        e, tok, g = blk
        h = x_pad[tok] @ w1[e] + b1[e]
        y = clamped_swiglu(h) @ w2[e] + b2[e]
        return acc.at[tok].add(y * g[:, None].astype(y.dtype)), None

    acc, _ = lax.scan(step, jnp.zeros((T + 1, D), xt.dtype),
                      (block_expert, row_tok.reshape(n_blocks, EXPERT_BLOCK),
                       row_gate.reshape(n_blocks, EXPERT_BLOCK)))
    return acc[:T].reshape(B, S, D)

def setup_inputs(seed: int = 0) -> dict:
    key = jax.random.key(seed)
    ks = jax.random.split(key, 24)
    L, D, E, I = DEPTH, D_MODEL, N_EXPERTS, D_EXPERT
    nrm = lambda k, shape, s: jax.random.normal(k, shape, jnp.float32) * s
    u = jax.random.uniform(ks[9], (L, LRU_W), jnp.float32, 0.9, 0.999)
    p = u ** (1.0 / LRU_C)
    return {
        "x": nrm(ks[0], (BATCH, SEQ, D), 1.0),
        "norm1_scale": 1.0 + nrm(ks[1], (L, D), 0.02),
        "w_in": nrm(ks[2], (L, D, IN_COLS), D ** -0.5),
        "f_bias": 2.0 + nrm(ks[3], (L, N_HEADS), 0.5),
        "gate_bias": nrm(ks[4], (L, N_BRANCHES * D), 0.02),
        "conv_w": nrm(ks[5], (L, CONV_W, LRU_W), CONV_W ** -0.5),
        "conv_b": nrm(ks[6], (L, LRU_W), 0.02),
        "rg_wa": nrm(ks[7], (L, N_LRU_BLOCKS, LRU_BLOCK, LRU_BLOCK), LRU_BLOCK ** -0.5),
        "rg_ba": nrm(ks[8], (L, N_LRU_BLOCKS, LRU_BLOCK), 0.02),
        "rg_wx": nrm(ks[10], (L, N_LRU_BLOCKS, LRU_BLOCK, LRU_BLOCK), LRU_BLOCK ** -0.5),
        "rg_bx": nrm(ks[11], (L, N_LRU_BLOCKS, LRU_BLOCK), 0.02),
        "rg_lambda": jnp.log(p / (1.0 - p)),
        "w_attn_proj": nrm(ks[12], (L, ATTN_W, D), ATTN_W ** -0.5),
        "w_rec_proj": nrm(ks[13], (L, LRU_W, D), LRU_W ** -0.5),
        "w_out": nrm(ks[14], (L, D, D), D ** -0.5),
        "norm2_scale": 1.0 + nrm(ks[15], (L, D), 0.02),
        "router_w": nrm(ks[16], (L, D, E), D ** -0.5),
        "router_b": nrm(ks[17], (L, E), 0.01),
        "moe_w1": nrm(ks[18], (L, E, D, 2 * I), D ** -0.5),
        "moe_b1": nrm(ks[19], (L, E, 2 * I), 0.02),
        "moe_w2": nrm(ks[20], (L, E, I, D), I ** -0.5),
        "moe_b2": nrm(ks[21], (L, E, D), 0.02),
        "final_norm_scale": 1.0 + nrm(ks[22], (D,), 0.02),
    }

def reference(x, norm1_scale, w_in, f_bias, gate_bias, conv_w, conv_b, rg_wa, rg_ba, rg_wx,
              rg_bx, rg_lambda, w_attn_proj, w_rec_proj, w_out, norm2_scale, router_w, router_b,
              moe_w1, moe_b1, moe_w2, moe_b2, final_norm_scale):
    for l in range(DEPTH):
        xn = rmsnorm(x, norm1_scale[l])
        x = x + hybrid_mixer(xn, w_in[l], f_bias[l], gate_bias[l], conv_w[l], conv_b[l],
                             rg_wa[l], rg_ba[l], rg_wx[l], rg_bx[l], rg_lambda[l],
                             w_attn_proj[l], w_rec_proj[l], w_out[l])
        xn = rmsnorm(x, norm2_scale[l])
        x = x + moe_ffn(xn, router_w[l], router_b[l], moe_w1[l], moe_b1[l], moe_w2[l], moe_b2[l])
    return rmsnorm(x, final_norm_scale)


_drawn_inputs = setup_inputs


def setup_inputs(seed=0):
    import zlib

    import numpy as np

    out = dict(_drawn_inputs(seed))
    spreads = {}
    factors = {'gate_bias': 10.237,
     'rg_ba': 15.421,
     'rg_bx': 10.443,
     'moe_b1': 5.281,
     'moe_b2': 6.088,
     'final_norm_scale': 22.706}
    for name, (base, spread) in spreads.items():
        noise = np.random.default_rng([zlib.crc32(name.encode()), seed]).standard_normal(out[name].shape)
        drawn = base * np.exp(spread * noise) if base else spread * noise
        out[name] = __import__('jax').numpy.asarray(drawn.astype(out[name].dtype))
    for name, factor in factors.items():
        out[name] = (out[name] * factor).astype(out[name].dtype)
    return out
```

```python
import concourse.bass as bass
from concourse import mybir
from contextlib import ExitStack

fp32 = mybir.dt.float32
fp32r = mybir.dt.float32r
i32 = mybir.dt.int32
u32 = mybir.dt.uint32
ALU = mybir.AluOpType
ACT = mybir.ActivationFunctionType
AXX = mybir.AxisListType.X

P = 128
T = 256
TT = T // P
D = 1024
DC = D // P
HEADS = 16
DH = 64
PAIRS = HEADS // 2
CONV = 4
E = 32
TOPK = 4
EP = E // 2
CAP = 64
MAX_ROUNDS = T // CAP
HID = 2 * D
EPS = 1e-6
ALPHA = 1.702
LIMIT = 7.0
LRU_C = 8.0
NEG = -1.0e30
NOT_HERE = -1000.0
GELU_A = 0.044715
GELU_C = 0.7978845608028654

NB = 512
R = 6
SLOT = 4096
RAW = 3
HI = 3
LOW_X = 5
SLOT_ORDER = (5, 2, 0, 3, 1, 4)
Q0, K0, V0 = 0, D, 2 * D
F0 = 3 * D
X0 = F0 + HEADS
Y0 = X0 + D
G0 = Y0 + D
CH_X, CH_Q, CH_K, CH_V, CH_Y, CH_G, CH_AP, CH_RP, CH_O = 0, 2, 4, 6, 8, 10, 14, 16, 18
MIX_CHUNKS = 20
W1_CHUNKS = DC
W2_CHUNKS = DC // 2
PAIR_CHUNKS = W1_CHUNKS + W2_CHUNKS
assert PAIR_CHUNKS == 2 * R
U_XNT, U_X, U_Q, U_K, U_V, U_Y, U_G, U_AP, U_RP, U_O, U_XNT2 = 0, 4, 8, 12, 16, 20, 24, 32, 36, 40, 44
MIX_USES = 48
PV_N1, PV_CW, PV_CB, PV_BA, PV_BX, PV_LAM, PV_GB, PV_ROWS = 0, 8, 40, 48, 56, 64, 72, 88
G0_PAIR, G1_PAIR = 5, 4
G0_ROUND, G1_ROUND = 1 + EP * G0_PAIR + 2, 1 + EP * G1_PAIR + 2


def build(nc, x, norm1_scale, w_in, f_bias, gate_bias, conv_w, conv_b, rg_wa, rg_ba, rg_wx, rg_bx,
          rg_lambda, w_attn_proj, w_rec_proj, w_out, norm2_scale, router_w, router_b,
          moe_w1, moe_b1, moe_w2, moe_b2, final_norm_scale, out):
    ctx = ExitStack()
    with ctx:
        def sb(name, shape, dt=fp32):
            return ctx.enter_context(nc.sbuf_tensor(name, shape, dt))

        def sem(name):
            return ctx.enter_context(nc.semaphore(name))

        def place(name, before_, shape):
            with ExitStack() as held:
                if before_:
                    held.enter_context(nc.sbuf_tensor(name + "_before", [P, before_], fp32))
                return held.enter_context(nc.sbuf_tensor(name, shape, fp32r))

        low_w = place("low_w", 0, [P, RAW, SLOT])
        high_w = place("high_w", HI * SLOT, [P, 2, SLOT])
        xnL = place("xnL", LOW_X * SLOT, [P, DC, T])
        ring = sb("ring", [P, R, SLOT])
        ROW = 2048
        xnH = place("xnH", 1 * ROW, [P, DC, T])
        recL = place("recL", 3 * ROW, [P, DC, T])
        mergedH = place("mergedH", 4 * ROW, [P, DC, T])
        mergedL = place("mergedL", 5 * ROW, [P, DC, T])
        recH = place("recH", 6 * ROW, [P, DC, T])
        attnH = place("attnH", 9 * ROW, [P, DC, T])
        attnL = place("attnL", 10 * ROW, [P, DC, T])
        arena = sb("arena", [P, 12, ROW])

        def row(n):
            return arena[:, n, :]

        def by_token(ap):
            return ap.rearrange("p (t d) -> p t d", t=TT)

        def by_chan(ap):
            return ap.rearrange("p (c t) -> p c t", c=DC)

        xs = by_token(row(0))
        xn = by_token(row(2))
        xc = by_chan(row(2))
        hT = by_chan(row(2))
        aT = by_chan(row(3))
        squares = by_token(row(3))
        gtmp = by_chan(row(3))
        pv = row(4)[0:PV_ROWS, 0:P]
        wf = row(5)[:, 0:DC * HEADS].rearrange("p (k h) -> p k h", k=DC)
        uT = by_chan(row(4))
        ixT = by_chan(row(5))
        wbd = row(6).rearrange("p (g c j) -> p g c j", g=2, c=DC)
        yT = by_chan(row(6))
        xp = arena[:, 7:9, :].rearrange("p a b -> p (a b)")[:, 0:DC * (T + CONV - 1)] \
            .rearrange("p (c t) -> p c t", c=DC)
        gA = by_chan(row(7))
        gR = by_chan(row(8))
        xnT = by_chan(row(9))
        qT = by_chan(row(9))
        kT = by_chan(row(10))
        vS = by_token(row(11))
        xn2 = by_token(row(2))
        xn2T = by_chan(row(1))
        yS = row(1)[:, 0:1024]
        actT = row(1)[:, 1024:2048].rearrange("p (c s) -> p c s", c=DC)
        xgT = row(3)[:, 0:1024].rearrange("p (c s) -> p c s", c=DC)
        actS = row(3)[:, 1024:2048]
        glu = row(4)[:, 0:1024]
        sig = row(4)[:, 1024:2048]
        lin = row(5)[:, 0:1024]
        gated = row(5)[:, 1024:2048]
        r6 = row(6)
        sel = r6[:, 0:256].rearrange("p (t s) -> p t s", t=TT)
        selG = r6[:, 256:512].rearrange("p (t s) -> p t s", t=TT)
        selGT = r6[:, 512:768].rearrange("p (t s) -> p t s", t=TT)
        oneh = r6[:, 768:1024].rearrange("p (t k e) -> p t k e", t=TT, k=TOPK)
        onehG = r6[:, 1024:1280].rearrange("p (t k e) -> p t k e", t=TT, k=TOPK)
        lg = r6[:, 1280:1344].rearrange("p (t e) -> p t e", t=TT)
        mask = r6[:, 1344:1408].rearrange("p (t e) -> p t e", t=TT)
        gateE = r6[:, 1408:1472].rearrange("p (t e) -> p t e", t=TT)
        posm = r6[:, 1472:1544].rearrange("p (t e) -> p t e", t=TT)
        top8 = r6[:, 1544:1560].rearrange("p (t k) -> p t k", t=TT)
        idx8 = r6[:, 1560:1576].rearrange("p (t k) -> p t k", t=TT).bitcast(u32)
        idxf = r6[:, 1576:1592].rearrange("p (t k) -> p t k", t=TT)
        gk = r6[:, 1592:1600].rearrange("p (t k) -> p t k", t=TT)
        rout = r6[:, 1600:1632]
        b1s = row(9)[0:2, :]
        b2s = row(10)[0:2, 0:D]
        rw = row(10)[:, D:D + DC * E].rearrange("p (k e) -> p k e", k=DC)
        rb = row(10)[:, D + DC * E:D + DC * E + E]
        n2b = row(11)[:, 0:D]
        fnb = row(11)[:, D:2 * D]

        ident = sb("ident", [P, P])
        causal = sb("causal", [P, 3, P])
        before = sb("before", [P, P])
        ones = sb("ones", [P, P])
        slot_no = sb("slot_no", [P, CAP])
        expert_no = sb("expert_no", [P, E])
        halves = sb("halves", [2, P])
        pvT = sb("pvT", [P, PV_ROWS])
        pvH = sb("pvH", [P, PV_ROWS])
        sp = sb("sp", [P, 3, DC])
        fb = sb("fb", [HEADS, 1])
        negc = sb("negc", [HEADS, T + P])
        stat = sb("stat", [P, 3 * TT])
        sumsq = sb("sumsq", [P, TT, 2])
        eps = sb("eps", [P, 1])
        probs = sb("probs", [P, 2, 2, 3 * P])
        ftmp = probs[0:HEADS, :, :, :].rearrange("p a b c -> p (a b c)")
        mx = sb("mx", [P, 2, 4])
        den = sb("den", [P, 2, 4])
        pT = sb("pT", [P, 2, 3 * P])
        rounds_i = sb("rounds_i", [P, 1], i32)

        bank = [ctx.enter_context(nc.psum_tensor(f"bank{i}", [P, NB], fp32)) for i in range(8)]
        H, G, Y = bank[0:4], bank[4:6], bank[6:8]

        slot_full = [sem(f"slot_full{i}") for i in range(R)]
        x_in, wf_in, pv_in, fb_in = [sem("x0_in"), sem("x1_in")], sem("wf_in"), sem("pv_in"), sem("fb_in")
        wbd_in, rw_in, rb_in, norms_in = sem("wbd_in"), sem("rw_in"), sem("rb_in"), sem("norms_in")
        b1_full, b2_full, out_done = sem("b1_full"), sem("b2_full"), sem("out_done")
        ident_ready, consts_ready, pool_step = sem("ident_ready"), sem("consts_ready"), sem("pool_step")
        low_odd = sem("low_odd")
        recL_ready = sem("recL_ready")
        wbd_zero, xp_zero, eps_ready = sem("wbd_zero"), sem("xp_zero"), sem("eps_ready")
        gelu_sq, gelu_arg, gated_ready = sem("gelu_sq"), sem("gelu_arg"), sem("gated_ready")
        w1_used, w2_used = sem("w1_used"), sem("w2_used")
        full = [sem(f"full{i}") for i in range(4)]
        free = [sem(f"free{i}") for i in range(4)]
        pv_full, f_full, gates_full, scores_full = sem("pv_full"), sem("f_full"), sem("gates_full"), sem("scores_full")
        pt_full, o_full = sem("pt_full"), sem("o_full")
        logits_full, pos_full = sem("logits_full"), sem("pos_full")
        b1_used, hidden_full, y_full = sem("b1_used"), sem("hidden_full"), sem("y_full")
        g_full = [sem("g0_full"), sem("g1_full")]
        act_step = sem("act_step")
        xnH_ready, high, recH_ready, mergedH_ready = sem("xnH_ready"), sem("high"), sem("recH_ready"), sem("mergedH_ready")
        std_ready, lam_l, f_l = sem("std_ready"), sem("lam_l"), sem("f_l")
        gates_read, lru_u, lru_i, lru_root = sem("gates_read"), sem("lru_u"), sem("lru_i"), sem("lru_root")
        exp_ready, pt_read, o_read, gelu_tanh = sem("exp_ready"), sem("pt_read"), sem("o_read"), sem("gelu_tanh")
        top_exp, sig_ready, y0_out = sem("top_exp"), sem("sig_ready"), sem("y0_out")
        dve_step = sem("dve_step")
        xnL_ready, low_even = sem("xnL_ready"), sem("low_even")
        attn_ready, summed, merged_ready = sem("attn_ready"), sem("summed"), sem("merged_ready")
        ms_ready, xn_ready, pvT_ready, sp_ready = sem("ms_ready"), sem("xn_ready"), sem("pvT_ready"), sem("sp_ready")
        negc_ready, xc_ready, lru_m, h_ready = sem("negc_ready"), sem("xc_ready"), sem("lru_m"), sem("h_ready")
        scores_read, negmx_ready, probs_ready = sem("scores_read"), sem("negmx_ready"), sem("probs_ready")
        gelu_lin, rec_ready = sem("gelu_lin"), sem("rec_ready")
        mask_ready, rounds_ready = sem("mask_ready"), sem("rounds_ready")
        scatter_empty = sem("scatter_empty")
        top_neg = sem("top_neg")
        sel_ready, selG_ready, posm_ready = sem("sel_ready"), sem("selG_ready"), sem("posm_ready")
        glu_ready, lin_ready, slots_eq, act_ready = sem("glu_ready"), sem("lin_ready"), sem("slots_eq"), sem("act_ready")
        y1_out, fin_ready = sem("y1_out"), sem("fin_ready")
        g_free = [sem("g0_free"), sem("g1_free")]

        def use(n):
            return n % 4, n // 4

        def wait_mix_chunk_used(eng, n):
            b, before_ = use(U_O + 2 + n - CH_O if n >= CH_O else U_X + 2 * n + 1)
            eng.wait_ge(full[b], before_ + 1)

        def wait_mix_half_used(eng, n, h):
            if CH_V <= n < CH_V + 2:
                wait_mix_chunk_used(eng, n)
            else:
                b, before_ = use(U_X + 2 * n + h)
                eng.wait_ge(full[b], before_ + 1)

        def chunk(n):
            return ring[:, n % RAW, :].rearrange("p (k n) -> p k n", k=DC)

        def w_high(n):
            return high_w[:, n % 2, :].rearrange("p (k n) -> p k n", k=DC)

        def w_low(n):
            return low_w[:, n % RAW, :].rearrange("p (k n) -> p k n", k=DC)

        def half_cols(u):
            return slice(u % 2 * 2 * P, (u % 2 + 1) * 2 * P)

        HALF_CHUNKS = 2 * MIX_CHUNKS

        def split_low(eng, engine, u, done):
            eng.wait_ge(high, u + 1)
            n, c = u // 2, half_cols(u)
            engine.tensor_tensor(w_low(n)[:, :, c], chunk(n)[:, :, c], w_high(n)[:, :, c], ALU.subtract) \
                  .then_inc(done, 1)

        def further_rounds(eng, body):
            eng.wait_ge(rounds_ready, 1)
            n = eng.value_load(rounds_i[0:1, 0:1], min_val=1, max_val=MAX_ROUNDS)
            with eng.If(n > 1):
                with eng.Fori(1, n) as r:
                    body(r)

        block = ctx.enter_context(nc.Block())

        @block.sync
        def _(sp_):
            for s in (glu_ready, lin_ready, act_ready, gated_ready, y0_out, y1_out):
                sp_.sem_inc(s, 1)
            for t in range(TT):
                sp_.dma_start(xs[:, t, :], x[0][t * P:(t + 1) * P, :]).then_inc(x_in[t], 16)

            def rows(first, count, src):
                sp_.dma_start(pv[first:first + count, :], src).then_inc(pv_in, 16)

            rows(PV_N1, DC, norm1_scale[0].rearrange("(c p) -> c p", p=P))
            rows(PV_CW, CONV * DC, conv_w[0].rearrange("j (c p) -> (j c) p", p=P))
            rows(PV_CB, DC, conv_b[0].rearrange("(c p) -> c p", p=P))
            rows(PV_BA, DC, rg_ba[0].rearrange("(c b) i -> c (b i)", b=2))
            rows(PV_BX, DC, rg_bx[0].rearrange("(c b) i -> c (b i)", b=2))
            rows(PV_LAM, DC, rg_lambda[0].rearrange("(c p) -> c p", p=P))
            rows(PV_GB, 2 * DC, gate_bias[0].rearrange("(c p) -> c p", p=P))
            sp_.dma_start(wf, w_in[0][:, F0:F0 + HEADS].rearrange("(k p) h -> p k h", p=P)).then_inc(wf_in, 16)
            sp_.dma_start(fb[:], f_bias.rearrange("a h -> h a")).then_inc(fb_in, 16)

            def mix_chunk(n, src):
                if n >= RAW:
                    wait_mix_chunk_used(sp_, n - RAW)
                sp_.dma_start(chunk(n), src.rearrange("(k p) n -> p k n", p=P)) \
                   .then_inc(slot_full[n % RAW], 16)

            for first, col, count in ((CH_X, X0, 2), (CH_Q, Q0, 2), (CH_K, K0, 2), (CH_V, V0, 2),
                                      (CH_Y, Y0, 2), (CH_G, G0, 4)):
                for j in range(count):
                    mix_chunk(first + j, w_in[0][:, col + j * NB:col + (j + 1) * NB])
                if first == CH_X:
                    sp_.wait_ge(wbd_zero, 1)
                    for g, w in enumerate((rg_wa, rg_wx)):
                        for b in range(2):
                            sp_.dma_start(wbd[b * 64:(b + 1) * 64, g, :, b * 64:(b + 1) * 64],
                                          w[0].rearrange("(c b) i j -> b i c j", b=2)[b]).then_inc(wbd_in, 16)
            for first, w in ((CH_AP, w_attn_proj), (CH_RP, w_rec_proj), (CH_O, w_out)):
                for j in range(2):
                    mix_chunk(first + j, w[0][:, j * NB:(j + 1) * NB])

            def load(j, i):
                s = SLOT_ORDER[j % R]
                if j < W1_CHUNKS:
                    sp_.dma_start(ring[:, s, :].rearrange("p (e n) -> p e n", e=2),
                                  moe_w1[0, bass.ds(i * 2, 2), j * P:(j + 1) * P, :]
                                  .rearrange("e p n -> p e n")).then_inc(slot_full[s], 16)
                    return
                k = 2 * (j - W1_CHUNKS)
                for e in range(2):
                    sp_.dma_start(ring[:, s, e * 2048:(e + 1) * 2048].rearrange("p (k n) -> p k n", k=2),
                                  moe_w2[0, bass.ds(i * 2 + e, 1), k * P:(k + 2) * P, :]
                                  .rearrange("e (k p) n -> p (e k) n", p=P)).then_inc(slot_full[s], 16)

            def wait_used(g, j):
                if j < W1_CHUNKS - 1:
                    sp_.wait_ge(w1_used, g * (W1_CHUNKS - 1) + (j + 1))
                elif j == W1_CHUNKS - 1:
                    sp_.wait_ge(hidden_full, g * 4 + 4)
                elif j < PAIR_CHUNKS - 1:
                    sp_.wait_ge(w2_used, g * (W2_CHUNKS - 1) + (j - W1_CHUNKS + 1))
                else:
                    sp_.wait_ge(y_full, g * 2 + 2)

            def load_round(r):
                if isinstance(r, int):
                    for j in range(R):
                        wait_mix_chunk_used(sp_, (CH_G + 3, 17, 18, 18, 19, 19)[j])
                        if j == 1:
                            sp_.dma_start(b1s, moe_b1[0, 0:2, :]).then_inc(b1_full, 16)
                            sp_.dma_start(b2s, moe_b2[0, 0:2, :]).then_inc(b2_full, 16)
                        load(j, 0)
                else:
                    sp_.wait_ge(b1_used, r * EP)
                    sp_.dma_start(b1s, moe_b1[0, 0:2, :]).then_inc(b1_full, 16)
                    wait_used(r * EP - 1, PAIR_CHUNKS - 1)
                    sp_.dma_start(b2s, moe_b2[0, 0:2, :]).then_inc(b2_full, 16)
                    for j in range(R):
                        load(j, 0)
                with sp_.Fori(0, EP - 1) as i:
                    g = sp_.snap(i + r * EP)
                    for j in range(R, PAIR_CHUNKS):
                        wait_used(g, j - R)
                        load(j, i)
                    sp_.wait_ge(b1_used, g + 1)
                    sp_.dma_start(b1s, moe_b1[0, bass.ds(i * 2 + 2, 2), :]).then_inc(b1_full, 16)
                    for j in range(R):
                        wait_used(g, PAIR_CHUNKS - R + j)
                        load(j, i + 1)
                        if j == R - 1 - W2_CHUNKS + 2:
                            sp_.dma_start(b2s, moe_b2[0, bass.ds(i * 2 + 2, 2), :]).then_inc(b2_full, 16)
                for j in range(R, PAIR_CHUNKS):
                    wait_used(r * EP + (EP - 1), j - R)
                    load(j, EP - 1)

            load_round(0)
            further_rounds(sp_, load_round)

        @block.gpsimd
        def _(pool):
            step = [0]

            def link(ins):
                step[0] += 1
                ins.then_inc(pool_step, 1)
                pool.wait_ge(pool_step, step[0])

            pl = nc.gpsimd
            link(pl.memset(ident[:], 0.0))
            pl.affine_select(out=ident[:], in_=ident[:], compare_op=ALU.not_equal, fill=1.0, base=0,
                             pattern=[[-1, P]], channel_multiplier=1).then_inc(ident_ready, 1)
            pl.memset(eps[:], EPS).then_inc(eps_ready, 1)
            pl.memset(row(6), 0.0).then_inc(wbd_zero, 1)
            pl.memset(xp[:, :, 0:CONV - 1], 0.0).then_inc(xp_zero, 1)
            pl.memset(ones[:], 1.0).then_inc(consts_ready, 1)
            link(pl.memset(causal[:], 0.0))
            for j in (0, 2):
                pl.affine_select(out=causal[:, j, :], in_=causal[:, j, :], compare_op=ALU.is_ge,
                                 fill=NEG, base=0, pattern=[[-1, P]], channel_multiplier=1) \
                  .then_inc(consts_ready, 1)
            pl.iota(slot_no[:], pattern=[[1, CAP]], base=0, channel_multiplier=0,
                    allow_small_or_imprecise_dtypes=True).then_inc(consts_ready, 1)
            pl.iota(expert_no[:], pattern=[[1, E]], base=0, channel_multiplier=0,
                    allow_small_or_imprecise_dtypes=True).then_inc(consts_ready, 1)
            link(pl.memset(before[:], 1.0))
            pl.affine_select(out=before[:], in_=before[:], compare_op=ALU.is_gt, fill=0.0, base=0,
                             pattern=[[1, P]], channel_multiplier=-1).then_inc(consts_ready, 1)
            link(pl.memset(halves[:], 1.0))
            link(pl.affine_select(out=halves[:], in_=halves[:], compare_op=ALU.is_ge, fill=0.0, base=0,
                                  pattern=[[1, P]], channel_multiplier=-CAP))
            pl.affine_select(out=halves[:], in_=halves[:], compare_op=ALU.is_gt, fill=0.0, base=CAP,
                             pattern=[[-1, P]], channel_multiplier=CAP).then_inc(consts_ready, 1)

            def low(u):
                if u % 2 and u < HALF_CHUNKS:
                    split_low(pool, pl, u, low_odd)

            def gelu_arg_out(n):
                c = slice(2 * n, 2 * n + 2)
                b, before_ = use(U_Y + n)
                pool.wait_ge(free[b], before_ + 1)
                pool.wait_ge(h_ready, DC)
                pl.tensor_tensor(gtmp[:, c, :], yT[:, c, :], yT[:, c, :], ALU.mult).then_inc(gelu_sq, 1)
                pool.wait_ge(gelu_lin, n + 1)
                pl.tensor_tensor(gtmp[:, c, :], gtmp[:, c, :], yT[:, c, :], ALU.mult).then_inc(gelu_arg, 1)

            for u in range(2 * CH_Y + 4):
                low(u)
            for s in range(12):
                if s < 4:
                    gelu_arg_out(s)
                if 2 <= s < 6:
                    c = slice(2 * (s - 2), 2 * (s - 2) + 2)
                    pool.wait_ge(recH_ready, s - 1)
                    pl.tensor_tensor(recL[:, c, :], hT[:, c, :], recH[:, c, :], ALU.subtract).then_inc(recL_ready, 1)
                low(2 * CH_Y + 4 + s)
            for u in range(2 * CH_AP + 4, HALF_CHUNKS):
                low(u)

            def gate_round(r):
                with pool.Fori(0, EP) as i:
                    g = pool.snap(i + r * EP)
                    for j in range(2):
                        c = slice(j * NB, (j + 1) * NB)
                        pool.wait_ge(sig_ready, g * 2 + (j + 1))
                        pool.wait_ge(act_ready, g * 2 + 1)
                        pl.tensor_tensor(gated[:, c], glu[:, c], sig[:, c], ALU.mult) \
                          .then_inc(gated_ready, 1)

            gate_round(0)
            further_rounds(pool, gate_round)

        @block.tensor
        def _(pe):
            mm, tr = nc.tensor.matmul, nc.tensor.transpose

            def split(u):
                pe.wait_ge(low_odd if u % 2 else low_even, u // 2 + 1)

            def mm3(out_, stationary, moving, start, stop):
                mm(out_, stationary[0], moving[0], start=start, stop=False)
                mm(out_, stationary[0], moving[1], start=False, stop=False)
                return mm(out_, stationary[1], moving[0], start=False, stop=stop)

            xn_parts = (xnH, xnL)

            pe.wait_ge(ident_ready, 1)
            pe.wait_ge(pv_in, 16 * 7)
            tr(bank[5][:, 0:PV_ROWS], pv[:, :], ident[0:PV_ROWS, 0:PV_ROWS]).then_inc(pv_full, 1)

            def transposed(n0, src):
                for n in range(4):
                    b, before_ = use(n0 + n)
                    if before_:
                        pe.wait_ge(free[b], before_)
                    for c in range(2):
                        for t in range(TT):
                            last = tr(bank[b][:, (c * TT + t) * P:(c * TT + t + 1) * P],
                                      src[:, t, (2 * n + c) * P:(2 * n + c + 1) * P], ident[:])
                    last.then_inc(full[b], 1)

            pe.wait_ge(xn_ready, TT)
            transposed(U_XNT, xn)

            for n in range(4):
                pe.wait_ge(free[n], 1)
            pe.wait_ge(wf_in, 16)
            for k in range(DC):
                last = mm(bank[4][0:HEADS, 0:T], wf[:, k, :], xnT[:, k, :], start=(k == 0), stop=(k == DC - 1))
            last.then_inc(f_full, 1)

            def columns(n0, n, ch0, src, part=(0, 1)):
                b, before_ = use(n0 + n)
                ch = ch0 + n // 2
                if 0 in part:
                    split(2 * ch0 + n)
                    pe.wait_ge(free[b], before_)
                for c in part:
                    col = (2 * (n % 2) + c) * P
                    for k in range(DC):
                        last = mm3(bank[b][:, c * T:(c + 1) * T],
                                   (w_high(ch)[:, k, col:col + P], w_low(ch)[:, k, col:col + P]),
                                   (src[0][:, k, :], src[1][:, k, :]), start=(k == 0), stop=(k == DC - 1))
                if 1 in part:
                    last.then_inc(full[b], 1)

            def token_rows(b, src, t, ch, ready=None):
                for k in range(DC):
                    if ready is not None and k % 2 == 0:
                        pe.wait_ge(ready, k // 2 + 1)
                    last = mm3(b[:, :], (src[0][:, k, t * P:(t + 1) * P], src[1][:, k, t * P:(t + 1) * P]),
                               (w_high(ch)[:, k, :], w_low(ch)[:, k, :]), start=(k == 0), stop=(k == DC - 1))
                return last

            def gates(c):
                pe.wait_ge(xc_ready, c + 1)
                if c >= 2:
                    pe.wait_ge(gates_read, c - 1)
                for g in range(2):
                    last = mm(bank[6 + c % 2][:, g * T:(g + 1) * T], wbd[:, g, c, :], xc[:, c, :],
                              start=True, stop=True)
                last.then_inc(gates_full, 1)

            pe.wait_ge(xnL_ready, 4)
            for n in range(4):
                columns(U_X, n, CH_X, xn_parts)
            pe.wait_ge(wbd_in, 16 * 4)
            for n in range(4):
                columns(U_Q, n, CH_Q, xn_parts)
                if n:
                    gates(n - 1)
            for n in range(4):
                columns(U_K, n, CH_K, xn_parts)
                gates(n + 3)
            for n in range(4):
                half, t = n // 2, n % 2
                b, before_ = use(U_V + n)
                for h in range(2):
                    split(2 * (CH_V + half) + h)
                pe.wait_ge(free[b], before_)
                last = token_rows(bank[b], xn_parts, t, CH_V + half)
                last.then_inc(full[b], 1)
                if n == 0:
                    gates(DC - 1)

            def scores(p):
                if p == 0:
                    pe.wait_ge(negc_ready, 1)
                    for n in range(4):
                        pe.wait_ge(free[use(U_K + n)[0]], use(U_K + n)[1] + 1)
                else:
                    pe.wait_ge(scores_read, 2 * p)
                for a in range(2):
                    h = 2 * p + a
                    mm(bank[4 + a][:, 0:3 * P], ident[0:HEADS, h:h + 1].to_broadcast([HEADS, P]), negc[:, :],
                       start=True, stop=False)
                for t in (1, 0):
                    for a in range(2):
                        rows = slice(DH * a, DH * (a + 1))
                        last = mm(bank[4 + a][:, t * P:t * P + (t + 1) * P], qT[rows, p, t * P:(t + 1) * P],
                                  kT[rows, p, 0:(t + 1) * P], start=False, stop=(t == 0))
                        if t == 0:
                            last.then_inc(scores_full, 1)

            def probs_transposed(p, a):
                pe.wait_ge(probs_ready, 2 * p + a + 1)
                if p or a:
                    pe.wait_ge(pt_read, 2 * p + a)
                for j in range(3):
                    last = tr(bank[6][:, j * P:(j + 1) * P], probs[:, p % 2, a, j * P:(j + 1) * P], ident[:])
                last.then_inc(pt_full, 1)

            def values(p, a):
                h = 2 * p + a
                rows = slice(DH * a, DH * (a + 1))
                pe.wait_ge(pt_read, 2 * p + a + 1)
                if p and a == 0:
                    pe.wait_ge(attn_ready, p)
                mm(bank[7][rows, 0:T], vS[:, 0, h * DH:(h + 1) * DH], pT[:, a, 0:T], start=True, stop=False)
                last = mm(bank[7][rows, P:T], vS[:, 1, h * DH:(h + 1) * DH], pT[:, a, T:3 * P],
                          start=False, stop=True)
                if a == 1:
                    last.then_inc(o_full, 1)

            for s in range(12):
                n0, n, ch0 = (U_Y, s, CH_Y) if s < 4 else (U_G, s - 4, CH_G)
                p = s - 1
                if s < PAIRS:
                    if s == 0:
                        pe.wait_ge(gates_read, DC)
                    scores(s)
                if 0 <= p < PAIRS:
                    if p == 0:
                        for m in range(4):
                            pe.wait_ge(free[use(U_V + m)[0]], use(U_V + m)[1] + 1)
                    probs_transposed(p, 0)
                columns(n0, n, ch0, xn_parts, part=(0,))
                if 0 <= p < PAIRS:
                    values(p, 0)
                    probs_transposed(p, 1)
                columns(n0, n, ch0, xn_parts, part=(1,))
                if 0 <= p < PAIRS:
                    values(p, 1)

            pe.wait_ge(attn_ready, PAIRS)
            for n in range(4):
                columns(U_AP, n, CH_AP, (attnH, attnL))
            pe.wait_ge(recL_ready, 4)
            for n in range(4):
                columns(U_RP, n, CH_RP, (recH, recL))
            def transposed2(t):
                for h in range(2):
                    b, before_ = use(U_XNT2 + 2 * t + h)
                    pe.wait_ge(free[b], before_)
                    pe.wait_ge(xn_ready, TT + 2 * t + h + 1)
                    for c in range(4):
                        last = tr(bank[b][:, c * P:(c + 1) * P], xn2[:, t, (4 * h + c) * P:(4 * h + c + 1) * P],
                                  ident[:])
                    last.then_inc(full[b], 1)

            def logits(t):
                for k in range(DC):
                    if k % 4 == 0:
                        b, before_ = use(U_XNT2 + 2 * t + k // 4)
                        pe.wait_ge(free[b], before_ + 1)
                    last = mm(bank[4 + 2 * t][:, 0:E], xn2T[:, k, t * P:(t + 1) * P], rw[:, k, :],
                              start=(k == 0), stop=(k == DC - 1))
                last.then_inc(logits_full, 1)

            for n in range(4):
                t, half = n // 2, n % 2
                b, before_ = use(U_O + n)
                if n == 3:
                    transposed2(0)
                for h in range(2):
                    split(2 * (CH_O + half) + h)
                pe.wait_ge(free[b], before_)
                last = token_rows(bank[b], (mergedH, mergedL), t, CH_O + half, merged_ready)
                last.then_inc(full[b], 1)

            pe.wait_ge(rw_in, 16)
            logits(0)
            transposed2(1)
            logits(1)
            pe.wait_ge(consts_ready, 7)
            pe.wait_ge(mask_ready, 1)
            mm(bank[7][:, 0:E], before[:], mask[:, 0, :], start=True, stop=True)
            mm(bank[7][:, E:2 * E], ones[:], mask[:, 0, :], start=True, stop=False)
            pe.wait_ge(mask_ready, 2)
            mm(bank[7][:, E:2 * E], before[:], mask[:, 1, :], start=False, stop=True)
            mm(bank[7][:, 2 * E:3 * E], ones[:], mask[:, 0, :], start=True, stop=False)
            mm(bank[7][:, 2 * E:3 * E], ones[:], mask[:, 1, :], start=False, stop=True).then_inc(pos_full, 1)

            def gather(number):
                pe.wait_ge(sel_ready, number)
                for j in range(2):
                    for c in range(4):
                        for t in range(TT):
                            last = mm(G[j][:, c * P:(c + 1) * P],
                                      xn2[:, t, (4 * j + c) * P:(4 * j + c + 1) * P], sel[:, t, :],
                                      start=(t == 0), stop=(t == TT - 1))
                    last.then_inc(g_full[j], 1)

            def scatter(uses):
                for n in range(4):
                    t, half = n // 2, n % 2
                    pe.wait_ge(g_free[half], uses[half] + t)
                    mm(G[half][:, :], selGT[:, t, :], yS[:, half * NB:(half + 1) * NB],
                       start=True, stop=True).then_inc(g_full[half], 1)

            def expert_round(r):
                u0, u1 = r * G0_ROUND, r * G1_ROUND
                if not isinstance(r, int):
                    pe.wait_ge(g_free[0], u0)
                    pe.wait_ge(g_free[1], u1)
                gather(r * (EP + 1) + 1)
                with pe.Fori(0, EP) as i:
                    g = pe.snap(i + r * EP)
                    a0 = u0 + 1 + i * G0_PAIR
                    a1 = u1 + 1 + i * G1_PAIR
                    pe.wait_ge(glu_ready, g * 2 + 1)
                    pe.wait_ge(lin_ready, g * 2 + 1)
                    pe.wait_ge(b1_full, g * 16 + 16)
                    for b in range(4):
                        for e in range(2):
                            s = slice(e * CAP, (e + 1) * CAP)
                            last = mm(H[b][s, :], halves[:, s], b1s[:, b * NB:(b + 1) * NB], start=True, stop=False)
                    last.then_inc(b1_used, 1)
                    pe.wait_ge(g_free[0], a0)
                    pe.wait_ge(g_free[1], a1)
                    for k in range(W1_CHUNKS):
                        s_ = SLOT_ORDER[k % R]
                        w = ring[:, s_, :].rearrange("p (e n) -> p e n", e=2)
                        pe.wait_ge(slot_full[s_], slot_fill(g, k))
                        for b in range(4):
                            for e in range(2):
                                s = slice(e * CAP, (e + 1) * CAP)
                                last = mm(H[b][s, :], xgT[:, k, s], w[:, e, b * NB:(b + 1) * NB],
                                          start=False, stop=(k == W1_CHUNKS - 1))
                            if k == W1_CHUNKS - 1:
                                last.then_inc(hidden_full, 1)
                        if k < W1_CHUNKS - 1:
                            last.then_inc(w1_used, 1)
                    gather(r * (EP + 1) + (i + 2))
                    pe.wait_ge(y0_out, g + 1)
                    pe.wait_ge(y1_out, g + 1)
                    pe.wait_ge(scatter_empty, r + 1)
                    scatter((a0 + 1, a1 + 1))
                    pe.wait_ge(selG_ready, g + 1)
                    pe.wait_ge(g_free[0], a0 + 3)
                    for t in range(TT):
                        last = tr(G[0][:, t * P:(t + 1) * P], selG[:, t, :], ident[:])
                    last.then_inc(g_full[0], 1)
                    for j in range(2):
                        pe.wait_ge(act_ready, g * 2 + (j + 2))
                        if j == 0:
                            pe.wait_ge(g_free[1], a1 + 3)
                        else:
                            pe.wait_ge(g_free[0], a0 + 4)
                        for c in range(4):
                            last = tr(G[1 - j][:, c * P:(c + 1) * P],
                                      actS[:, (4 * j + c) * P:(4 * j + c + 1) * P], ident[:])
                        last.then_inc(g_full[1 - j], 1)
                    pe.wait_ge(b2_full, g * 16 + 16)
                    for half in range(2):
                        for e in range(2):
                            s = slice(e * CAP, (e + 1) * CAP)
                            mm(Y[half][s, :], halves[:, s], b2s[:, half * NB:(half + 1) * NB], start=True, stop=False)
                    pe.wait_ge(g_free[1], a1 + 4)
                    for m in range(W2_CHUNKS):
                        s_ = SLOT_ORDER[(W1_CHUNKS + m) % R]
                        w = ring[:, s_, :].rearrange("p (e k n) -> p e k n", e=2, k=2)
                        pe.wait_ge(slot_full[s_], slot_fill(g, W1_CHUNKS + m))
                        if m == 2:
                            pe.wait_ge(g_free[0], a0 + 5)
                        for kk in range(2):
                            k = 2 * m + kk
                            for half in range(2):
                                for e in range(2):
                                    s = slice(e * CAP, (e + 1) * CAP)
                                    last = mm(Y[half][s, :], actT[:, k, s], w[:, e, kk, half * NB:(half + 1) * NB],
                                              start=False, stop=(k == DC - 1))
                                if k == DC - 1:
                                    last.then_inc(y_full, 1)
                        if m < W2_CHUNKS - 1:
                            last.then_inc(w2_used, 1)
                done = (r + 1) * EP
                pe.wait_ge(y0_out, done + 1)
                pe.wait_ge(y1_out, done + 1)
                scatter((u0 + 1 + EP * G0_PAIR, u1 + 1 + EP * G1_PAIR))

            def slot_fill(g, j):
                s = SLOT_ORDER[j % R]
                mix = len([n for n in range(MIX_CHUNKS) if n % RAW == s])
                per = [16 if m < W1_CHUNKS else 32 for m in range(PAIR_CHUNKS) if SLOT_ORDER[m % R] == s]
                upto = sum((16 if m < W1_CHUNKS else 32) for m in range(j + 1) if SLOT_ORDER[m % R] == s)
                return g * sum(per) + (16 * mix + upto)

            for n in range(4):
                pe.wait_ge(free[n], MIX_USES // 4)
            expert_round(0)
            further_rounds(pe, expert_round)

        @block.scalar
        def _(act):
            step = [0]
            fn = nc.scalar.activation

            def link(ins):
                step[0] += 1
                ins.then_inc(act_step, 1)
                act.wait_ge(act_step, step[0])

            def root(k, t):
                act.wait_ge(ms_ready, TT * k + t + 1)
                fn(stat[:, TT + t:TT + t + 1], stat[:, t:t + 1], ACT.Sqrt, bias=eps[:, 0:1]).then_inc(std_ready, 1)

            act.wait_ge(eps_ready, 1)
            for t in range(TT):
                root(0, t)
            act.wait_ge(pvT_ready, 1)
            link(fn(sp[:, 0, :], pvT[:, PV_LAM:PV_LAM + DC], ACT.Abs))
            link(fn(sp[:, 0, :], sp[:, 0, :], ACT.Exp, scale=-1.0))
            fn(sp[:, 0, :], sp[:, 0, :], ACT.Ln, bias=1.0).then_inc(lam_l, 1)
            for n in (0, 2):
                b, before_ = use(U_XNT + n)
                act.wait_ge(full[b], before_ + 1)
                for c in range(2):
                    last = fn(xnT[:, 2 * n + c, :], bank[b][:, c * T:(c + 1) * T], ACT.Copy,
                              scale=pvT[:, PV_N1 + 2 * n + c:PV_N1 + 2 * n + c + 1])
                last.then_inc(free[b], 1)
            for n in range(4):
                act.wait_ge(free[n], 1)
                c = slice(2 * n, 2 * n + 2)
                fn(xnH[:, c, :], xnT[:, c, :], ACT.Copy).then_inc(xnH_ready, 1)

            def split_high(u):
                if u >= HALF_CHUNKS:
                    return
                n, c = u // 2, half_cols(u)
                act.wait_ge(slot_full[n % RAW], 16 * (n // RAW + 1))
                if n >= 2:
                    wait_mix_half_used(act, n - 2, u % 2)
                fn(w_high(n)[:, :, c], chunk(n)[:, :, c], ACT.Copy).then_inc(high, 1)

            for u in range(4):
                split_high(u)
            act.wait_ge(f_full, 1)
            act.wait_ge(fb_in, 16)
            link(fn(ftmp[:, 0:T], bank[4][0:HEADS, 0:T], ACT.Abs, bias=fb[:, 0:1]))
            link(fn(ftmp[:, 0:T], ftmp[:, 0:T], ACT.Exp, scale=-1.0))
            fn(ftmp[:, 0:T], ftmp[:, 0:T], ACT.Ln, bias=1.0).then_inc(f_l, 1)

            act.wait_ge(xp_zero, 1)

            def out_of_bank(n, dst, **how):
                b, before_ = use(n)
                act.wait_ge(full[b], before_ + 1)
                fn(dst, bank[b][:, :].rearrange("p (c t) -> p c t", c=2), ACT.Copy, **how).then_inc(free[b], 1)

            for n in range(4):
                out_of_bank(U_X + n, xp[:, 2 * n:2 * n + 2, CONV - 1:])
                split_high(2 * CH_X + n + 4)

            def gates(c):
                act.wait_ge(gates_full, c + 1)
                if c == 0:
                    act.wait_ge(sp_ready, 1)
                z = bank[6 + c % 2]
                link(fn(aT[:, c, :], z[:, 0:T], ACT.Tanh, bias=pvH[:, PV_BA + c:PV_BA + c + 1], scale=0.5))
                fn(ixT[:, c, :], z[:, T:2 * T], ACT.Tanh, bias=pvH[:, PV_BX + c:PV_BX + c + 1],
                   scale=0.5).then_inc(gates_read, 1)
                link(fn(uT[:, c, :], aT[:, c, :], ACT.Tanh, bias=sp[:, 1, c:c + 1], scale=sp[:, 1, c:c + 1]))
                fn(aT[:, c, :], aT[:, c, :], ACT.Exp, bias=sp[:, 2, c:c + 1],
                   scale=sp[:, 2, c:c + 1]).then_inc(lru_u, 1)

            for n in range(4):
                out_of_bank(U_Q + n, qT[:, 2 * n:2 * n + 2, :], scale=DH ** -0.5)
                split_high(2 * CH_Q + n + 4)
                if n:
                    gates(n - 1)
            for n in range(4):
                gates(n + 3)
                split_high(2 * CH_K + n + 4)
            for n in range(4):
                half, t = n // 2, n % 2
                b, before_ = use(U_V + n)
                act.wait_ge(full[b], before_ + 1)
                fn(vS[:, t, half * NB:(half + 1) * NB], bank[b][:, :], ACT.Copy).then_inc(free[b], 1)
                if n == 0:
                    gates(DC - 1)
                if t == 1:
                    for h in range(2):
                        split_high(2 * (CH_V + half) + h + 4)
                if n == 1:
                    act.wait_ge(lru_m, DC)
                    fn(uT, uT, ACT.Sqrt, scale=0.5).then_inc(lru_root, 1)

            def pt_out(p, a):
                act.wait_ge(pt_full, 2 * p + a + 1)
                if p:
                    act.wait_ge(o_full, p)
                fn(pT[:, a, :], bank[6][:, 0:3 * P], ACT.Copy).then_inc(pt_read, 1)

            for s in range(12):
                p = s - 1
                if 0 <= p < PAIRS:
                    pt_out(p, 0)
                if s < PAIRS:
                    for a in range(2):
                        act.wait_ge(negmx_ready, 2 * s + a + 1)
                        for t in range(2):
                            cols = slice(t * P, t * P + (t + 1) * P)
                            m = 2 * a + t
                            last = fn(probs[:, s % 2, a, cols], probs[:, s % 2, a, cols], ACT.Exp,
                                      bias=mx[:, s % 2, m:m + 1], accum_out=den[:, s % 2, m:m + 1])
                            last.then_inc(exp_ready, 1)
                if 0 <= p < PAIRS:
                    pt_out(p, 1)
                if s < 4:
                    if s == 0:
                        act.wait_ge(gates_full, DC)
                    out_of_bank(U_Y + s, yT[:, 2 * s:2 * s + 2, :])
                else:
                    n = s - 4
                    b, before_ = use(U_G + n)
                    act.wait_ge(full[b], before_ + 1)
                    if n == 0:
                        act.wait_ge(xc_ready, DC)
                    for c in range(2):
                        k = 2 * n + c
                        last = fn((gA if k < DC else gR)[:, k % DC, :], bank[b][:, c * T:(c + 1) * T], ACT.Tanh,
                                  bias=pvH[:, PV_GB + k:PV_GB + k + 1], scale=0.5)
                    last.then_inc(free[b], 1)
                if 1 <= s <= 4:
                    n = s - 1
                    act.wait_ge(gelu_arg, n + 1)
                    fn(gtmp[:, 2 * n:2 * n + 2, :], gtmp[:, 2 * n:2 * n + 2, :], ACT.Tanh,
                       scale=GELU_C).then_inc(gelu_tanh, 1)
                if 0 <= p < PAIRS:
                    act.wait_ge(o_full, p + 1)
                    fn(attnH[:, p, :], bank[7][:, 0:T], ACT.Copy).then_inc(o_read, 1)
                if 1 <= s <= 4:
                    c = slice(2 * (s - 1), 2 * (s - 1) + 2)
                    act.wait_ge(rec_ready, s)
                    fn(recH[:, c, :], hT[:, c, :], ACT.Copy).then_inc(recH_ready, 1)
                split_high(2 * CH_Y + s + 4)

            for n in range(4):
                split_high(2 * CH_AP + n + 4)
            wait_mix_chunk_used(act, CH_AP + 1)
            act.dma_start(rw, router_w[0].rearrange("(k p) e -> p k e", p=P)).then_inc(rw_in, 16)
            act.dma_start(rb[:], router_b[0].partition_broadcast(P)).then_inc(rb_in, 16)
            act.dma_start(n2b, norm2_scale[0].partition_broadcast(P)).then_inc(norms_in, 16)
            act.dma_start(fnb, final_norm_scale.partition_broadcast(P)).then_inc(norms_in, 16)

            for n in range(4):
                c = slice(2 * n, 2 * n + 2)
                split_high(2 * CH_RP + n + 4)
                act.wait_ge(summed, n + 1)
                fn(mergedH[:, c, :], gA[:, c, :], ACT.Copy).then_inc(mergedH_ready, 1)

            def xn2T_out(t):
                b, before_ = use(U_XNT2 + 2 * t)
                act.wait_ge(full[b], before_ + 1)
                fn(xn2T[:, 0:4, t * P:(t + 1) * P], bank[b][:, :].rearrange("p (c t) -> p c t", c=4),
                   ACT.Copy).then_inc(free[b], 1)

            root(1, 0)
            xn2T_out(0)
            root(1, 1)
            xn2T_out(1)
            for t in range(TT):
                act.wait_ge(top_neg, t + 1)
                fn(gk[:, t, :], top8[:, t, 0:TOPK], ACT.Exp, bias=rout[:, t:t + 1],
                   accum_out=rout[:, 2 + t:3 + t]).then_inc(top_exp, 1)

            def gather_out(uses):
                for j in range(2):
                    act.wait_ge(g_full[j], uses[j] + 1)
                    fn(xgT[:, 4 * j:4 * j + 4, :], G[j][:, :].rearrange("p (c s) -> p c s", c=4),
                       ACT.Copy).then_inc(g_free[j], 1)

            def expert_round(r):
                u0, u1 = r * G0_ROUND, r * G1_ROUND
                gather_out((u0, u1))
                with act.Fori(0, EP) as i:
                    g = act.snap(i + r * EP)
                    a0 = u0 + 1 + i * G0_PAIR
                    a1 = u1 + 1 + i * G1_PAIR
                    for j in range(2):
                        c = slice(j * NB, (j + 1) * NB)
                        act.wait_ge(glu_ready, g * 2 + (j + 2))
                        act.wait_ge(gated_ready, g * 2 + 1)
                        fn(sig[:, c], glu[:, c], ACT.Sigmoid, scale=ALPHA).then_inc(sig_ready, 1)
                    gather_out((a0, a1))
                    act.wait_ge(g_full[0], a0 + 4)
                    fn(selGT, G[0][:, 0:2 * P].rearrange("p (t s) -> p t s", t=TT), ACT.Copy).then_inc(g_free[0], 1)
                    for j in range(2):
                        act.wait_ge(g_full[1 - j], (a1 + 4) if j == 0 else (a0 + 5))
                        fn(actT[:, 4 * j:4 * j + 4, :], G[1 - j][:, :].rearrange("p (c s) -> p c s", c=4),
                           ACT.Copy).then_inc(g_free[1 - j], 1)
                    act.wait_ge(y_full, g * 2 + 1)
                    fn(yS[:, 0:NB], Y[0][:, :], ACT.Copy).then_inc(y0_out, 1)

            expert_round(0)
            further_rounds(act, expert_round)

            for t in range(TT):
                root(2, t)
            for n in range(2 * TT):
                t, cols = n // 2, slice((n % 2) * NB, (n % 2 + 1) * NB)
                act.wait_ge(fin_ready, n + 1)
                act.dma_start(out[0, t * P:(t + 1) * P, cols], xn2[:, t, cols]).then_inc(out_done, 16)
            act.wait_ge(out_done, 16 * 2 * TT)

        @block.vector
        def _(dve):
            step = [0]
            v = nc.vector

            def link(ins):
                step[0] += 1
                ins.then_inc(dve_step, 1)
                dve.wait_ge(dve_step, step[0])

            def half(n):
                return slice(n * NB, (n + 1) * NB)

            def square_sum(t, h):
                link(v.tensor_tensor_reduce(out=squares[:, t, half(h)], in0=xs[:, t, half(h)], in1=xs[:, t, half(h)],
                                            scale=1.0, scalar=0.0, op0=ALU.mult, op1=ALU.add,
                                            accum_out=sumsq[:, t, h:h + 1]))

            def mean_square(t):
                v.tensor_scalar(stat[:, t:t + 1], sumsq[:, t, 0:1], sumsq[:, t, 1:2], 1.0 / D,
                                ALU.add, ALU.mult).then_inc(ms_ready, 1)

            def inv_rms(k, t):
                dve.wait_ge(std_ready, TT * k + t + 1)
                link(v.reciprocal(stat[:, 2 * TT + t:2 * TT + t + 1], stat[:, TT + t:TT + t + 1]))
                return stat[:, 2 * TT + t:2 * TT + t + 1]

            for t in range(TT):
                dve.wait_ge(x_in[t], 16)
                for h in range(2):
                    square_sum(t, h)
                mean_square(t)
            for t in range(TT):
                v.tensor_scalar(xn[:, t, :], xs[:, t, :], inv_rms(0, t), None, ALU.mult).then_inc(xn_ready, 1)
            dve.wait_ge(pv_full, 1)
            v.tensor_copy(pvT[:], bank[5][:, 0:PV_ROWS]).then_inc(pvT_ready, 1)
            dve.wait_ge(pvT_ready, 1)
            link(v.tensor_scalar(pvH[:], pvT[:], 0.5, None, ALU.mult))
            link(v.tensor_scalar(sp[:, 1, :], pvT[:, PV_LAM:PV_LAM + DC], -1.0, 0.0, ALU.mult, ALU.max))
            dve.wait_ge(lam_l, 1)
            link(v.tensor_tensor(sp[:, 1, :], sp[:, 1, :], sp[:, 0, :], ALU.add))
            link(v.tensor_scalar(sp[:, 1, :], sp[:, 1, :], LRU_C / 2, None, ALU.mult))
            v.tensor_scalar(sp[:, 2, :], sp[:, 1, :], -1.0, None, ALU.mult).then_inc(sp_ready, 1)
            for n in (1, 3):
                b, before_ = use(U_XNT + n)
                dve.wait_ge(full[b], before_ + 1)
                for c in range(2):
                    last = v.tensor_scalar(xnT[:, 2 * n + c, :], bank[b][:, c * T:(c + 1) * T],
                                           pvT[:, PV_N1 + 2 * n + c:PV_N1 + 2 * n + c + 1], None, ALU.mult)
                last.then_inc(free[b], 1)
            for n in range(4):
                dve.wait_ge(xnH_ready, n + 1)
                c = slice(2 * n, 2 * n + 2)
                v.tensor_tensor(xnL[:, c, :], xnT[:, c, :], xnH[:, c, :], ALU.subtract).then_inc(xnL_ready, 1)

            def low(u):
                if u % 2 == 0 and u < HALF_CHUNKS:
                    split_low(dve, v, u, low_even)

            low(0)
            low(2)
            dve.wait_ge(f_l, 1)
            link(v.tensor_scalar(ftmp[:, T:2 * T], bank[4][0:HEADS, 0:T], fb[:, 0:1], 0.0, ALU.add, ALU.min))
            link(v.tensor_tensor(ftmp[:, 0:T], ftmp[:, 0:T], ftmp[:, T:2 * T], ALU.subtract))
            link(v.memset(ftmp[:, T:2 * T], 1.0))
            link(v.tensor_tensor_scan(negc[:, P:P + T], ftmp[:, T:2 * T], ftmp[:, 0:T], 0.0, ALU.mult, ALU.add))
            v.tensor_copy(negc[:, 0:P], negc[:, P:2 * P]).then_inc(negc_ready, 1)

            def conv(c):
                w = [pvT[:, PV_CW + j * DC + c:PV_CW + j * DC + c + 1] for j in range(CONV)]
                link(v.tensor_scalar(xc[:, c, :], xp[:, c, 0:T], w[0], pvT[:, PV_CB + c:PV_CB + c + 1],
                                     ALU.mult, ALU.add))
                for j in range(1, CONV):
                    ins = v.scalar_tensor_tensor(xc[:, c, :], xp[:, c, j:j + T], w[j], xc[:, c, :], ALU.mult, ALU.add)
                    if j < CONV - 1:
                        link(ins)
                    else:
                        ins.then_inc(xc_ready, 1)

            def lru_gates(c):
                dve.wait_ge(lru_u, c + 1)
                v.scalar_tensor_tensor(ixT[:, c, :], ixT[:, c, :], 1.0, xc[:, c, :], ALU.add, ALU.mult) \
                 .then_inc(lru_i, 1)
                dve.wait_ge(lru_i, c + 1)
                link(v.tensor_scalar(xc[:, c, :], uT[:, c, :], 1.0, None, ALU.add))
                link(v.reciprocal(xc[:, c, :], xc[:, c, :]))
                v.scalar_tensor_tensor(uT[:, c, :], uT[:, c, :], 1e-30, xc[:, c, :], ALU.max, ALU.mult) \
                 .then_inc(lru_m, 1)

            def k_out(n):
                b, before_ = use(U_K + n)
                dve.wait_ge(full[b], before_ + 1)
                v.tensor_copy(kT[:, 2 * n:2 * n + 2, :], bank[b][:, :].rearrange("p (c t) -> p c t", c=2)) \
                 .then_inc(free[b], 1)

            for c in range(DC):
                if c % 2 == 0:
                    b, before_ = use(U_X + c // 2)
                    dve.wait_ge(free[b], before_ + 1)
                conv(c)
                if c % 2 == 1:
                    low(2 * CH_X + c // 2 + 4)
            low(2 * CH_Q + 4)
            for c in range(3):
                lru_gates(c)
                low(2 * CH_Q + c + 5)
            for n in range(4):
                k_out(n)
                lru_gates(n + 3)
                low(2 * CH_K + n + 4)
            lru_gates(DC - 1)
            low(2 * CH_V + 4)
            dve.wait_ge(lru_root, 1)
            link(v.memset(uT[:, :, 0:1], 0.5))
            link(v.tensor_tensor(row(5), row(4), row(5), ALU.mult))
            for c in range(DC):
                v.tensor_tensor_scan(hT[:, c, :], aT[:, c, :], ixT[:, c, :], 0.0, ALU.mult, ALU.add).then_inc(h_ready, 1)
            low(2 * CH_V + 6)

            def softmax(p):
                q = p % 2
                if p == 0:
                    dve.wait_ge(consts_ready, 7)
                for a in range(2):
                    dve.wait_ge(scores_full, 2 * p + a + 1)
                    if p >= 2:
                        dve.wait_ge(pt_full, 2 * (p - 2) + a + 1)
                    for t in range(2):
                        cols = slice(t * P, t * P + (t + 1) * P)
                        m = 2 * a + t
                        last = v.tensor_tensor_reduce(
                            out=probs[:, q, a, cols], in0=bank[4 + a][:, cols],
                            in1=causal[:, :, :].rearrange("p a b -> p (a b)")[:, cols], scale=1.0,
                            scalar=NEG, op0=ALU.add, op1=ALU.max, accum_out=mx[:, q, m:m + 1])
                    last.then_inc(scores_read, 1)
                    dve.wait_ge(scores_read, 2 * p + a + 1)
                    v.tensor_scalar(mx[:, q, 2 * a:2 * a + 2], mx[:, q, 2 * a:2 * a + 2], -1.0, None,
                                    ALU.mult).then_inc(negmx_ready, 1)
                for a in range(2):
                    dve.wait_ge(exp_ready, 4 * p + 2 * a + 2)
                    link(v.reciprocal(den[:, q, 2 * a:2 * a + 2], den[:, q, 2 * a:2 * a + 2]))
                    for t in range(2):
                        cols = slice(t * P, t * P + (t + 1) * P)
                        m = 2 * a + t
                        last = v.tensor_scalar(probs[:, q, a, cols], probs[:, q, a, cols],
                                               den[:, q, m:m + 1], None, ALU.mult)
                    last.then_inc(probs_ready, 1)

            def gelu_in(n):
                c = slice(2 * n, 2 * n + 2)
                dve.wait_ge(gelu_sq, n + 1)
                v.tensor_scalar(gtmp[:, c, :], gtmp[:, c, :], GELU_A, 1.0, ALU.mult, ALU.add).then_inc(gelu_lin, 1)

            def gelu_out(n):
                c = slice(2 * n, 2 * n + 2)
                dve.wait_ge(gelu_tanh, n + 1)
                link(v.scalar_tensor_tensor(yT[:, c, :], gtmp[:, c, :], 1.0, yT[:, c, :], ALU.add, ALU.mult))
                v.scalar_tensor_tensor(hT[:, c, :], hT[:, c, :], 0.5, yT[:, c, :], ALU.mult, ALU.mult) \
                 .then_inc(rec_ready, 1)

            for s in range(12):
                if s < PAIRS:
                    softmax(s)
                if s < 4:
                    gelu_in(s)
                if 1 <= s <= 4:
                    gelu_out(s - 1)
                if 1 <= s <= PAIRS:
                    dve.wait_ge(o_read, s)
                    v.tensor_tensor(attnL[:, s - 1, :], bank[7][:, 0:T], attnH[:, s - 1, :], ALU.subtract) \
                     .then_inc(attn_ready, 1)
                low(2 * CH_Y + s + 4)

            def gate_product(g_, n0, n):
                c = slice(2 * n, 2 * n + 2)
                b, before_ = use(n0 + n)
                dve.wait_ge(full[b], before_ + 1)
                v.scalar_tensor_tensor(g_[:, c, :], g_[:, c, :], 1.0,
                                       bank[b][:, :].rearrange("p (c t) -> p c t", c=2),
                                       ALU.add, ALU.mult).then_inc(free[b], 1)
                return b, before_

            for n in range(4):
                gate_product(gA, U_AP, n)
                low(2 * CH_AP + n + 4)
            for n in range(4):
                c = slice(2 * n, 2 * n + 2)
                b, before_ = gate_product(gR, U_RP, n)
                dve.wait_ge(free[b], before_ + 1)
                v.tensor_tensor(gA[:, c, :], gA[:, c, :], gR[:, c, :], ALU.add).then_inc(summed, 1)
                if n < 3:
                    low(2 * CH_RP + n + 4)
                dve.wait_ge(mergedH_ready, n + 1)
                v.tensor_tensor(mergedL[:, c, :], gA[:, c, :], mergedH[:, c, :], ALU.subtract).then_inc(merged_ready, 1)
            def x1(t):
                for h in range(2):
                    b, before_ = use(U_O + 2 * t + h)
                    dve.wait_ge(full[b], before_ + 1)
                    v.scalar_tensor_tensor(xs[:, t, half(h)], bank[b][:, :], 0.5, xs[:, t, half(h)],
                                           ALU.mult, ALU.add).then_inc(free[b], 1)
                    dve.wait_ge(free[b], before_ + 1)
                    square_sum(t, h)
                mean_square(t)
                inv = inv_rms(1, t)
                for h in range(2):
                    v.scalar_tensor_tensor(xn2[:, t, half(h)], xs[:, t, half(h)], inv, n2b[:, half(h)],
                                           ALU.mult, ALU.mult).then_inc(xn_ready, 1)

            def xn2T_out(t):
                b, before_ = use(U_XNT2 + 2 * t + 1)
                dve.wait_ge(full[b], before_ + 1)
                v.tensor_copy(xn2T[:, 4:8, t * P:(t + 1) * P], bank[b][:, :].rearrange("p (c t) -> p c t", c=4)) \
                 .then_inc(free[b], 1)

            def choose(t):
                dve.wait_ge(logits_full, t + 1)
                link(v.tensor_tensor(lg[:, t, :], bank[4 + 2 * t][:, 0:E], rb[:, :], ALU.add))
                link(v.max(out=top8[:, t, :], in_=lg[:, t, :]))
                link(v.max_index(out=idx8[:, t, :], in_max=top8[:, t, :], in_values=lg[:, t, :]))
                v.tensor_scalar(rout[:, t:t + 1], top8[:, t, 0:1], -1.0, None, ALU.mult).then_inc(top_neg, 1)
                link(v.tensor_copy(idxf[:, t, :], idx8[:, t, :]))
                link(v.tensor_tensor(oneh[:, t], expert_no[:, :].unsqueeze(1).to_broadcast([P, TOPK, E]),
                                     idxf[:, t, 0:TOPK].unsqueeze(2).to_broadcast([P, TOPK, E]), ALU.is_equal))
                v.tensor_reduce(mask[:, t, :], oneh[:, t].rearrange("p k e -> p e k"), AXX, ALU.add) \
                 .then_inc(mask_ready, 1)

            dve.wait_ge(norms_in, 32)
            dve.wait_ge(rb_in, 16)
            link(v.memset(posm, NOT_HERE))
            x1(0)
            xn2T_out(0)
            x1(1)
            choose(0)
            xn2T_out(1)
            choose(1)
            dve.wait_ge(pos_full, 1)
            link(v.scalar_tensor_tensor(posm[:, :, 0:E], mask, -NOT_HERE,
                                        bank[7][:, 0:TT * E].rearrange("p (t e) -> p t e", t=TT), ALU.mult, ALU.add))
            v.tensor_scalar(posm[:, :, 0:E], posm[:, :, 0:E], NOT_HERE, None, ALU.add).then_inc(posm_ready, 1)

            def gates_and_rounds():
                dve.wait_ge(top_exp, TT)
                link(v.reciprocal(rout[:, 4:6], rout[:, 2:4]))
                link(v.tensor_tensor(gk, gk, rout[:, 4:6].unsqueeze(2).to_broadcast([P, TT, TOPK]), ALU.mult))
                link(v.tensor_tensor(onehG, oneh, gk.unsqueeze(3).to_broadcast([P, TT, TOPK, E]), ALU.mult))
                link(v.tensor_reduce(gateE, onehG.rearrange("p t k e -> p t e k"), AXX, ALU.add))
                link(v.tensor_reduce(rout[:, 6:7], bank[7][:, TT * E:(TT + 1) * E], AXX, ALU.max))
                link(v.tensor_scalar(rout[:, 8:9], rout[:, 6:7], float(CAP), None, ALU.is_gt))
                link(v.tensor_scalar(rout[:, 9:10], rout[:, 6:7], float(2 * CAP), None, ALU.is_gt))
                link(v.tensor_scalar(rout[:, 10:11], rout[:, 6:7], float(3 * CAP), 1.0, ALU.is_gt, ALU.add))
                link(v.tensor_reduce(rout[:, 7:8], rout[:, 8:11], AXX, ALU.add))
                v.tensor_copy(rounds_i[:], rout[:, 7:8]).then_inc(rounds_ready, 1)

            numbers = slot_no[:, :].unsqueeze(1).unsqueeze(1).to_broadcast([P, TT, 2, CAP])
            sel4 = sel.rearrange("p t (e s) -> p t e s", e=2)
            selG4 = selG.rearrange("p t (e s) -> p t e s", e=2)

            def of_pair(table, first):
                return table[:, :, bass.ds(first, 2)].unsqueeze(3).to_broadcast([P, TT, 2, CAP])

            def expert_round(r):
                u0, u1 = r * G0_ROUND, r * G1_ROUND
                if not isinstance(r, int):
                    dve.wait_ge(g_free[0], u0)
                    dve.wait_ge(g_free[1], u1)
                    v.tensor_scalar(posm, posm, -float(CAP), None, ALU.add).then_inc(posm_ready, 1)
                dve.wait_ge(posm_ready, r + 1)
                v.tensor_tensor(sel4, numbers, of_pair(posm, 0), ALU.is_equal).then_inc(sel_ready, 1)
                if isinstance(r, int):
                    link(v.memset(yS, 0.0))
                v.memset(selGT, 0.0).then_inc(scatter_empty, 1)
                if isinstance(r, int):
                    gates_and_rounds()

                def add_back(uses):
                    for n in range(4):
                        t, half = n // 2, n % 2
                        cols = slice(half * NB, (half + 1) * NB)
                        dve.wait_ge(g_full[half], uses[half] + (t + 1))
                        v.tensor_tensor(xs[:, t, cols], G[half][:, :], xs[:, t, cols], ALU.add) \
                         .then_inc(g_free[half], 1)

                with dve.Fori(0, EP) as i:
                    g = dve.snap(i + r * EP)
                    a0 = u0 + 1 + i * G0_PAIR
                    a1 = u1 + 1 + i * G1_PAIR
                    i2 = i * 2
                    dve.wait_ge(g_full[0], a0)
                    dve.wait_ge(g_full[1], a1)
                    v.tensor_tensor(selG4, numbers, of_pair(posm, i2), ALU.is_equal).then_inc(slots_eq, 1)
                    dve.wait_ge(slots_eq, g + 1)
                    v.tensor_tensor(selG4, selG4, of_pair(gateE, i2), ALU.mult).then_inc(selG_ready, 1)
                    v.tensor_tensor(sel4, numbers, of_pair(posm, i2 + 2), ALU.is_equal).then_inc(sel_ready, 1)
                    for j in range(2):
                        c = slice(j * NB, (j + 1) * NB)
                        dve.wait_ge(hidden_full, g * 4 + (j + 1))
                        v.tensor_scalar(glu[:, c], H[j][:, :], LIMIT, None, ALU.min).then_inc(glu_ready, 1)
                        dve.wait_ge(hidden_full, g * 4 + (j + 3))
                        v.tensor_scalar(lin[:, c], H[2 + j][:, :], -LIMIT, LIMIT, ALU.max, ALU.min) \
                         .then_inc(lin_ready, 1)
                    for j in range(2):
                        c = slice(j * NB, (j + 1) * NB)
                        dve.wait_ge(gated_ready, g * 2 + (j + 2))
                        dve.wait_ge(lin_ready, g * 2 + (j + 2))
                        v.scalar_tensor_tensor(actS[:, c], lin[:, c], 1.0, gated[:, c], ALU.add, ALU.mult) \
                         .then_inc(act_ready, 1)
                    add_back((a0 + 1, a1 + 1))
                    dve.wait_ge(y_full, g * 2 + 2)
                    v.tensor_copy(yS[:, NB:2 * NB], Y[1][:, :]).then_inc(y1_out, 1)
                add_back((u0 + 1 + EP * G0_PAIR, u1 + 1 + EP * G1_PAIR))

            expert_round(0)
            further_rounds(dve, expert_round)

            for t in range(TT):
                for h in range(2):
                    square_sum(t, h)
                mean_square(t)
            for t in range(TT):
                inv = inv_rms(2, t)
                for h in range(2):
                    v.scalar_tensor_tensor(xn2[:, t, half(h)], xs[:, t, half(h)], inv, fnb[:, half(h)],
                                           ALU.mult, ALU.mult).then_inc(fin_ready, 1)


_INS = ["x", "norm1_scale", "w_in", "f_bias", "gate_bias", "conv_w", "conv_b", "rg_wa", "rg_ba", "rg_wx",
        "rg_bx", "rg_lambda", "w_attn_proj", "w_rec_proj", "w_out", "norm2_scale", "router_w", "router_b",
        "moe_w1", "moe_b1", "moe_w2", "moe_b2", "final_norm_scale"]


def kernel(**inputs):
    import numpy as np
    import concourse.bacc as bacc
    from concourse.bass_utils import run_bass_kernel_spmd

    nc = bacc.Bacc("TRN2", target_bir_lowering=False, num_devices=1)
    arrays, args = {}, []
    for name in _INS:
        a = np.ascontiguousarray(inputs[name])
        arrays[f"in_{name}"] = a
        args.append(nc.dram_tensor(f"in_{name}", a.shape, mybir.dt.from_np(a.dtype), kind="ExternalInput").ap())
    args.append(nc.dram_tensor("out_y", (1, T, D), fp32, kind="ExternalOutput").ap())
    build(nc, *args)
    r = run_bass_kernel_spmd(nc, [arrays], core_ids=[0])
    return r.results[0]["out_y"]
```

```python
import concourse.bass as bass
from concourse import mybir
from contextlib import ExitStack

fp32 = mybir.dt.float32
fp32r = mybir.dt.float32r
i32 = mybir.dt.int32
u32 = mybir.dt.uint32
ALU = mybir.AluOpType
ACT = mybir.ActivationFunctionType
AXX = mybir.AxisListType.X

P = 128
T = 256
TT = T // P
D = 1024
DC = D // P
HEADS = 16
DH = 64
PAIRS = HEADS // 2
CONV = 4
E = 32
TOPK = 4
EP = E // 2
CAP = 64
MAX_ROUNDS = T // CAP
HID = 2 * D
EPS = 1e-6
ALPHA = 1.702
LIMIT = 7.0
LRU_C = 8.0
NEG = -1.0e30
NOT_HERE = -1000.0
GELU_A = 0.044715
GELU_C = 0.7978845608028654

NB = 512
R = 6
SLOT = 4096
RAW = 3
HI = 3
LOW_X = 5
SLOTS = 8
Q0, K0, V0 = 0, D, 2 * D
F0 = 3 * D
X0 = F0 + HEADS
Y0 = X0 + D
G0 = Y0 + D
CH_X, CH_Q, CH_K, CH_V, CH_Y, CH_G, CH_AP, CH_RP, CH_O = 0, 2, 4, 6, 8, 10, 14, 16, 18
MIX_CHUNKS = 20
Y_STEPS, G_STEPS = (0, 1, 4, 5), (2, 3, 6, 7, 8, 9, 10, 11)
STEPS = len(Y_STEPS) + len(G_STEPS)
W1_CHUNKS = DC
W2_CHUNKS = DC // 2
PAIR_CHUNKS = W1_CHUNKS + W2_CHUNKS
TWO = 2 * PAIR_CHUNKS
assert TWO % SLOTS == 0
SLOT_OF = [(5, 7, 2, 6, 0, 3, 1, 4)[n % SLOTS] for n in range(TWO)]
U_XNT, U_X, U_Q, U_K, U_V, U_Y, U_G, U_AP, U_RP, U_O, U_XNT2 = 0, 4, 8, 12, 16, 20, 24, 32, 36, 40, 44
MIX_USES = 48
PV_N1, PV_CW, PV_CB, PV_BA, PV_BX, PV_LAM, PV_GB, PV_ROWS = 0, 8, 40, 48, 56, 64, 72, 88
G0_PAIR, G1_PAIR = 5, 4
G0_ROUND, G1_ROUND = 1 + EP * G0_PAIR + 2, 1 + EP * G1_PAIR + 2


def build(nc, x, norm1_scale, w_in, f_bias, gate_bias, conv_w, conv_b, rg_wa, rg_ba, rg_wx, rg_bx,
          rg_lambda, w_attn_proj, w_rec_proj, w_out, norm2_scale, router_w, router_b,
          moe_w1, moe_b1, moe_w2, moe_b2, final_norm_scale, out):
    ctx = ExitStack()
    with ctx:
        def sb(name, shape, dt=fp32):
            return ctx.enter_context(nc.sbuf_tensor(name, shape, dt))

        def sem(name):
            return ctx.enter_context(nc.semaphore(name))

        def place(name, before_, shape):
            with ExitStack() as held:
                if before_:
                    held.enter_context(nc.sbuf_tensor(name + "_before", [P, before_], fp32))
                return held.enter_context(nc.sbuf_tensor(name, shape, fp32r))

        low_w = place("low_w", 0, [P, RAW, SLOT])
        high_w = place("high_w", HI * SLOT, [P, 2, SLOT])
        xnL = place("xnL", LOW_X * SLOT, [P, DC, T])
        ring = sb("ring", [P, R, SLOT])
        ROW = 2048
        xnH = place("xnH", 1 * ROW, [P, DC, T])
        recL = place("recL", 3 * ROW, [P, DC, T])
        mergedH = place("mergedH", 4 * ROW, [P, DC, T])
        mergedL = place("mergedL", 5 * ROW, [P, DC, T])
        recH = place("recH", 6 * ROW, [P, DC, T])
        attnH = place("attnH", 9 * ROW, [P, DC, T])
        attnL = place("attnL", 10 * ROW, [P, DC, T])
        arena = sb("arena", [P, 12, ROW])

        def row(n):
            return arena[:, n, :]

        def by_token(ap):
            return ap.rearrange("p (t d) -> p t d", t=TT)

        def by_chan(ap):
            return ap.rearrange("p (c t) -> p c t", c=DC)

        xs = by_token(row(0))
        xn = by_token(row(2))
        xc = by_chan(row(2))
        hT = by_chan(row(2))
        aT = by_chan(row(3))
        squares = by_token(row(3))
        gtmp = by_chan(row(3))
        pv = row(4)[0:PV_ROWS, 0:P]
        wf = row(5)[:, 0:DC * HEADS].rearrange("p (k h) -> p k h", k=DC)
        uT = by_chan(row(4))
        ixT = by_chan(row(5))
        wbd = row(6).rearrange("p (g c j) -> p g c j", g=2, c=DC)
        yT = by_chan(row(6))
        xp = arena[:, 7:9, :].rearrange("p a b -> p (a b)")[:, 0:DC * (T + CONV - 1)] \
            .rearrange("p (c t) -> p c t", c=DC)
        gA = by_chan(row(7))
        gR = by_chan(row(8))
        xnT = by_chan(row(9))
        qT = by_chan(row(9))
        kT = by_chan(row(10))
        vS = by_token(row(11))
        xn2 = by_token(row(2))
        xn2T = by_chan(row(1))
        yS = row(1)[:, 0:1024]
        actT = row(1)[:, 1024:2048].rearrange("p (c s) -> p c s", c=DC)
        xgT = row(3)[:, 0:1024].rearrange("p (c s) -> p c s", c=DC)
        actS = row(3)[:, 1024:2048]
        glu = row(4)[:, 0:1024]
        sig = row(4)[:, 1024:2048]
        lin = row(5)[:, 0:1024]
        gated = row(5)[:, 1024:2048]
        r6 = row(6)
        sel = r6[:, 0:256].rearrange("p (t s) -> p t s", t=TT)
        selG = r6[:, 256:512].rearrange("p (t s) -> p t s", t=TT)
        selGT = r6[:, 512:768].rearrange("p (t s) -> p t s", t=TT)
        oneh = r6[:, 768:1024].rearrange("p (t k e) -> p t k e", t=TT, k=TOPK)
        onehG = r6[:, 1024:1280].rearrange("p (t k e) -> p t k e", t=TT, k=TOPK)
        lg = r6[:, 1280:1344].rearrange("p (t e) -> p t e", t=TT)
        mask = r6[:, 1344:1408].rearrange("p (t e) -> p t e", t=TT)
        gateE = r6[:, 1408:1472].rearrange("p (t e) -> p t e", t=TT)
        posm = r6[:, 1472:1544].rearrange("p (t e) -> p t e", t=TT)
        top8 = r6[:, 1544:1560].rearrange("p (t k) -> p t k", t=TT)
        idx8 = r6[:, 1560:1576].rearrange("p (t k) -> p t k", t=TT).bitcast(u32)
        idxf = r6[:, 1576:1592].rearrange("p (t k) -> p t k", t=TT)
        gk = r6[:, 1592:1600].rearrange("p (t k) -> p t k", t=TT)
        rout = r6[:, 1600:1632]
        n2b = row(11)[:, 0:D]
        fnb = row(11)[:, 0:D]
        b1s = row(11)[0:8, D:D + NB]
        b2s = row(11)[32:36, D:D + NB]
        rw = row(11)[:, D + NB:D + NB + DC * E].rearrange("p (k e) -> p k e", k=DC)
        rb = row(11)[:, D + NB + DC * E:D + NB + DC * E + E]

        ident = sb("ident", [P, P])
        causal = sb("causal", [P, 3, P])
        before = sb("before", [P, P])
        ones = sb("ones", [P, P])
        slot_no = sb("slot_no", [P, CAP])
        expert_no = sb("expert_no", [P, E])
        pvT = sb("pvT", [P, PV_ROWS])
        pvH = sb("pvH", [P, PV_ROWS])
        sp = sb("sp", [P, 3, DC])
        fb = sb("fb", [HEADS, 1])
        negc_parts = ctx.enter_context(nc.sbuf_tensor("negc_parts", [P, T + P], fp32r))
        head_rows = ctx.enter_context(nc.sbuf_tensor("head_rows", [P, HEADS], fp32r))
        stat = sb("stat", [P, 3 * TT])
        sumsq = sb("sumsq", [P, TT, 2])
        eps = sb("eps", [P, 1])
        probs = sb("probs", [P, 2, 2, 3 * P])
        ftmp = probs[0:HEADS, :, :, :].rearrange("p a b c -> p (a b c)")
        negc = ftmp[:, 2 * T:2 * T + T + P]
        mx = sb("mx", [P, 2, 4])
        den = sb("den", [P, 2, 4])
        pT = sb("pT", [P, 2, 3 * P])
        rounds_i = sb("rounds_i", [P, 1], i32)

        bank = [ctx.enter_context(nc.psum_tensor(f"bank{i}", [P, NB], fp32)) for i in range(8)]
        H, G, Y = bank[0:4], bank[4:6], bank[6:8]

        slot_full = [sem(f"slot_full{i}") for i in range(SLOTS)]
        x_in, wf_in, pv_in, fb_in = [sem("x0_in"), sem("x1_in")], sem("wf_in"), sem("pv_in"), sem("fb_in")
        wbd_in, rw_in, rb_in, norms_in, final_in = sem("wbd_in"), sem("rw_in"), sem("rb_in"), sem("norms_in"), sem("final_in")
        b1_full, b2_full, out_done = sem("b1_full"), sem("b2_full"), sem("out_done")
        ident_ready, consts_ready, pool_step = sem("ident_ready"), sem("consts_ready"), sem("pool_step")
        low_odd = sem("low_odd")
        recL_ready, scaled = sem("recL_ready"), sem("scaled")
        rows_zero = sem("rows_zero")
        wbd_zero, xp_zero, eps_ready = sem("wbd_zero"), sem("xp_zero"), sem("eps_ready")
        gelu_sq, gelu_arg, gated_ready = sem("gelu_sq"), sem("gelu_arg"), sem("gated_ready")
        w1_used, w2_used = sem("w1_used"), sem("w2_used")
        full = [sem(f"full{i}") for i in range(4)]
        free = [sem(f"free{i}") for i in range(4)]
        pv_full, f_full, gates_full, scores_full = sem("pv_full"), sem("f_full"), sem("gates_full"), sem("scores_full")
        pt_full, o_full = sem("pt_full"), sem("o_full")
        logits_full, pos_full = sem("logits_full"), sem("pos_full")
        b1_used, hidden_full, y_full = sem("b1_used"), sem("hidden_full"), sem("y_full")
        g_full = [sem("g0_full"), sem("g1_full")]
        act_step = sem("act_step")
        xnH_ready, high, recH_ready, mergedH_ready = sem("xnH_ready"), sem("high"), sem("recH_ready"), sem("mergedH_ready")
        std_ready, lam_l, f_l = sem("std_ready"), sem("lam_l"), sem("f_l")
        gates_read, lru_u, lru_i, lru_root = sem("gates_read"), sem("lru_u"), sem("lru_i"), sem("lru_root")
        exp_ready, pt_read, o_read, gelu_tanh = sem("exp_ready"), sem("pt_read"), sem("o_read"), sem("gelu_tanh")
        top_exp, sig_ready, y0_out, fin_ready = sem("top_exp"), sem("sig_ready"), sem("y0_out"), [sem("fin0_ready"), sem("fin1_ready")]
        dve_step = sem("dve_step")
        xnL_ready, low_even = sem("xnL_ready"), sem("low_even")
        attn_ready, summed, merged_ready = sem("attn_ready"), sem("summed"), sem("merged_ready")
        ms_ready, xn_ready, pvT_ready, sp_ready = sem("ms_ready"), sem("xn_ready"), sem("pvT_ready"), sem("sp_ready")
        negc_ready, xc_ready, lru_m, h_ready = sem("negc_ready"), sem("xc_ready"), sem("lru_m"), sem("h_ready")
        scores_read, negmx_ready, probs_ready = sem("scores_read"), sem("negmx_ready"), sem("probs_ready")
        gelu_lin, rec_ready = sem("gelu_lin"), sem("rec_ready")
        mask_ready, rounds_ready = sem("mask_ready"), sem("rounds_ready")
        scatter_empty = sem("scatter_empty")
        top_neg = sem("top_neg")
        sel_ready, selG_ready, posm_ready = sem("sel_ready"), sem("selG_ready"), sem("posm_ready")
        glu_ready, lin_ready, slots_eq, act_ready = sem("glu_ready"), sem("lin_ready"), sem("slots_eq"), sem("act_ready")
        y1_out, inv_ready, summed_up = sem("y1_out"), sem("inv_ready"), sem("summed_up")
        g_free = [sem("g0_free"), sem("g1_free")]

        def use(n):
            return n % 4, n // 4

        def wait_mix_chunk_used(eng, n):
            b, before_ = use(U_O + 2 + n - CH_O if n >= CH_O else U_X + 2 * n + 1)
            eng.wait_ge(full[b], before_ + 1)

        def wait_mix_half_used(eng, n, h):
            if CH_V <= n < CH_V + 2:
                wait_mix_chunk_used(eng, n)
            else:
                b, before_ = use(U_X + 2 * n + h)
                eng.wait_ge(full[b], before_ + 1)

        def chunk(n):
            return ring[:, n % RAW, :].rearrange("p (k n) -> p k n", k=DC)

        def w_high(n):
            return high_w[:, n % 2, :].rearrange("p (k n) -> p k n", k=DC)

        def w_low(n):
            return low_w[:, n % RAW, :].rearrange("p (k n) -> p k n", k=DC)

        def expert_slot(odd, j):
            n = SLOT_OF[odd * PAIR_CHUNKS + j]
            return ring[:, n, :] if n < R else \
                arena[:, 2 * n - 5:2 * n - 3, :].rearrange("p a b -> p (a b)")

        def load_biases(eng, table, dst, first, done):
            eng.dma_start(dst, table[0, first, :].rearrange("e (b n) -> (e b) n", n=NB)).then_inc(done, 16)

        def half_cols(u):
            return slice(u % 2 * 2 * P, (u % 2 + 1) * 2 * P)

        HALF_CHUNKS = 2 * MIX_CHUNKS

        def split_low(eng, engine, u, done):
            eng.wait_ge(high, u + 1)
            n, c = u // 2, half_cols(u)
            engine.tensor_tensor(w_low(n)[:, :, c], chunk(n)[:, :, c], w_high(n)[:, :, c], ALU.subtract) \
                  .then_inc(done, 1)

        def further_rounds(eng, body):
            eng.wait_ge(rounds_ready, 1)
            n = eng.value_load(rounds_i[0:1, 0:1], min_val=1, max_val=MAX_ROUNDS)
            with eng.If(n > 1):
                with eng.Fori(1, n) as r:
                    body(r)

        block = ctx.enter_context(nc.Block())

        @block.sync
        def _(sp_):
            for s in (glu_ready, lin_ready, act_ready, gated_ready, y0_out, y1_out):
                sp_.sem_inc(s, 1)
            for t in range(TT):
                sp_.dma_start(xs[:, t, :], x[0][t * P:(t + 1) * P, :]).then_inc(x_in[t], 16)

            def rows(first, count, src):
                sp_.dma_start(pv[first:first + count, :], src).then_inc(pv_in, 16)

            rows(PV_N1, DC, norm1_scale[0].rearrange("(c p) -> c p", p=P))
            rows(PV_CW, CONV * DC, conv_w[0].rearrange("j (c p) -> (j c) p", p=P))
            rows(PV_CB, DC, conv_b[0].rearrange("(c p) -> c p", p=P))
            rows(PV_BA, DC, rg_ba[0].rearrange("(c b) i -> c (b i)", b=2))
            rows(PV_BX, DC, rg_bx[0].rearrange("(c b) i -> c (b i)", b=2))
            rows(PV_LAM, DC, rg_lambda[0].rearrange("(c p) -> c p", p=P))
            rows(PV_GB, 2 * DC, gate_bias[0].rearrange("(c p) -> c p", p=P))
            sp_.dma_start(wf, w_in[0][:, F0:F0 + HEADS].rearrange("(k p) h -> p k h", p=P)).then_inc(wf_in, 16)
            sp_.dma_start(fb[:], f_bias.rearrange("a h -> h a")).then_inc(fb_in, 16)

            def mix_chunk(n, src):
                if n >= RAW:
                    wait_mix_chunk_used(sp_, n - RAW)
                sp_.dma_start(chunk(n), src.rearrange("(k p) n -> p k n", p=P)) \
                   .then_inc(slot_full[n % RAW], 16)

            columns_of = [X0, X0 + NB, Q0, Q0 + NB, K0, K0 + NB, V0, V0 + NB]
            for s in range(0, STEPS, 2):
                columns_of.append(Y0 + Y_STEPS.index(s) * 2 * P if s in Y_STEPS else
                                  G0 + G_STEPS.index(s) * 2 * P)
            for first, col in enumerate(columns_of):
                mix_chunk(first, w_in[0][:, col:col + NB])
                if first == CH_X + 1:
                    sp_.wait_ge(wbd_zero, 1)
                    for g, w in enumerate((rg_wa, rg_wx)):
                        for b in range(2):
                            sp_.dma_start(wbd[b * 64:(b + 1) * 64, g, :, b * 64:(b + 1) * 64],
                                          w[0].rearrange("(c b) i j -> b i c j", b=2)[b]).then_inc(wbd_in, 16)
            for first, w in ((CH_AP, w_attn_proj), (CH_RP, w_rec_proj), (CH_O, w_out)):
                for j in range(2):
                    mix_chunk(first + j, w[0][:, j * NB:(j + 1) * NB])

            def load(j, i, odd):
                s, dst = SLOT_OF[odd * PAIR_CHUNKS + j], expert_slot(odd, j)
                if j < W1_CHUNKS:
                    sp_.dma_start(dst.rearrange("p (e n) -> p e n", e=2),
                                  moe_w1[0, bass.ds(i * 2, 2), j * P:(j + 1) * P, :]
                                  .rearrange("e p n -> p e n")).then_inc(slot_full[s], 16)
                    return
                k = 2 * (j - W1_CHUNKS)
                for e in range(2):
                    sp_.dma_start(dst[:, e * 2048:(e + 1) * 2048].rearrange("p (k n) -> p k n", k=2),
                                  moe_w2[0, bass.ds(i * 2 + e, 1), k * P:(k + 2) * P, :]
                                  .rearrange("e (k p) n -> p (e k) n", p=P)).then_inc(slot_full[s], 16)

            def wait_used(g, j):
                if j < W1_CHUNKS - 1:
                    sp_.wait_ge(w1_used, g * (W1_CHUNKS - 1) + (j + 1))
                elif j == W1_CHUNKS - 1:
                    sp_.wait_ge(hidden_full, g * 4 + 4)
                elif j < PAIR_CHUNKS - 1:
                    sp_.wait_ge(w2_used, g * (W2_CHUNKS - 1) + (j - W1_CHUNKS + 1))
                else:
                    sp_.wait_ge(y_full, g * 2 + 2)

            def wait_slot(g, j):
                if j >= SLOTS:
                    wait_used(g, j - SLOTS)
                else:
                    wait_used(g - 1, j + PAIR_CHUNKS - SLOTS)

            def pair_number(r, ii, odd):
                i = ii * 2 + odd
                g = i + r * EP
                return (g if isinstance(g, int) else sp_.snap(g)), i

            def load_rest(r, ii, odd, next_i=None):
                g, i = pair_number(r, ii, odd)
                sp_.wait_ge(b1_used, g + 1)
                load_biases(sp_, moe_b1, b1s, bass.ds(i * 2 + 2, 2) if next_i is None else slice(0, 2), b1_full)
                for j in range(SLOTS, PAIR_CHUNKS):
                    wait_slot(g, j)
                    load(j, i, odd)

            def load_first(r, ii, odd):
                g, i = pair_number(r, ii, odd)
                for j in range(SLOTS):
                    wait_slot(g + 1, j)
                    load(j, i + 1, 1 - odd)
                    if j + PAIR_CHUNKS - SLOTS == W1_CHUNKS:
                        load_biases(sp_, moe_b2, b2s, bass.ds(i * 2 + 2, 2), b2_full)

            def load_round(r):
                if isinstance(r, int):
                    for j in range(SLOTS):
                        if j == 3:
                            sp_.wait_ge(merged_ready, 4)
                        else:
                            wait_mix_chunk_used(sp_, (CH_G + 3, CH_AP + 1, 17, None, 18, 18, 19, 19)[j])
                        if j == 1:
                            load_biases(sp_, moe_b1, b1s, slice(0, 2), b1_full)
                            load_biases(sp_, moe_b2, b2s, slice(0, 2), b2_full)
                        load(j, 0, 0)
                else:
                    wait_used(r * EP - 1, PAIR_CHUNKS - 1)
                    load_biases(sp_, moe_b2, b2s, slice(0, 2), b2_full)
                    for j in range(SLOTS):
                        load(j, 0, 0)
                with sp_.Fori(0, EP // 2 - 1) as ii:
                    for odd in range(2):
                        load_rest(r, ii, odd)
                        load_first(r, ii, odd)
                load_rest(r, EP // 2 - 1, 0)
                load_first(r, EP // 2 - 1, 0)
                load_rest(r, EP // 2 - 1, 1, next_i=0)

            load_round(0)
            further_rounds(sp_, load_round)

            for n in range(2 * TT):
                t, cols = n // 2, slice((n % 2) * NB, (n % 2 + 1) * NB)
                sp_.wait_ge(fin_ready[t], n % 2 + 1)
                sp_.dma_start(out[0, t * P:(t + 1) * P, cols], xn2[:, t, cols]).then_inc(out_done, 16)
            sp_.wait_ge(out_done, 16 * 2 * TT)

        @block.gpsimd
        def _(pool):
            step = [0]

            def link(ins):
                step[0] += 1
                ins.then_inc(pool_step, 1)
                pool.wait_ge(pool_step, step[0])

            pl = nc.gpsimd
            link(pl.memset(ident[:], 0.0))
            pl.affine_select(out=ident[:], in_=ident[:], compare_op=ALU.not_equal, fill=1.0, base=0,
                             pattern=[[-1, P]], channel_multiplier=1).then_inc(ident_ready, 1)
            pl.memset(eps[:], EPS).then_inc(eps_ready, 1)
            pl.memset(row(6), 0.0).then_inc(wbd_zero, 1)
            pl.memset(negc_parts[:].bitcast(fp32), 0.0).then_inc(rows_zero, 1)
            pl.memset(head_rows[:].bitcast(fp32), 0.0).then_inc(rows_zero, 1)
            pl.memset(xp[:, :, 0:CONV - 1], 0.0).then_inc(xp_zero, 1)
            pl.memset(ones[:], 1.0).then_inc(consts_ready, 1)
            link(pl.memset(causal[:], 0.0))
            for j in (0, 2):
                pl.affine_select(out=causal[:, j, :], in_=causal[:, j, :], compare_op=ALU.is_ge,
                                 fill=NEG, base=0, pattern=[[-1, P]], channel_multiplier=1) \
                  .then_inc(consts_ready, 1)
            pl.iota(slot_no[:], pattern=[[1, CAP]], base=0, channel_multiplier=0,
                    allow_small_or_imprecise_dtypes=True).then_inc(consts_ready, 1)
            pl.iota(expert_no[:], pattern=[[1, E]], base=0, channel_multiplier=0,
                    allow_small_or_imprecise_dtypes=True).then_inc(consts_ready, 1)
            link(pl.memset(before[:], 1.0))
            pl.affine_select(out=before[:], in_=before[:], compare_op=ALU.is_gt, fill=0.0, base=0,
                             pattern=[[1, P]], channel_multiplier=-1).then_inc(consts_ready, 1)

            def low(u):
                if u % 2 and u < HALF_CHUNKS:
                    split_low(pool, pl, u, low_odd)

            def gelu_arg_out(n):
                c = slice(2 * n, 2 * n + 2)
                b, before_ = use(U_Y + Y_STEPS[n])
                pool.wait_ge(free[b], before_ + 1)
                pool.wait_ge(h_ready, DC)
                pl.tensor_tensor(gtmp[:, c, :], yT[:, c, :], yT[:, c, :], ALU.mult).then_inc(gelu_sq, 1)
                pool.wait_ge(gelu_lin, n + 1)
                pl.tensor_tensor(gtmp[:, c, :], gtmp[:, c, :], yT[:, c, :], ALU.mult).then_inc(gelu_arg, 1)

            for u in range(2 * CH_Y + 4):
                low(u)
            for s in range(STEPS):
                if s in Y_STEPS:
                    gelu_arg_out(Y_STEPS.index(s))
                if s - 2 in Y_STEPS:
                    n = Y_STEPS.index(s - 2)
                    c = slice(2 * n, 2 * n + 2)
                    pool.wait_ge(recH_ready, n + 1)
                    pl.tensor_tensor(recL[:, c, :], hT[:, c, :], recH[:, c, :], ALU.subtract).then_inc(recL_ready, 1)
                low(2 * CH_Y + 4 + s)
            for u in range(2 * CH_AP + 4, HALF_CHUNKS):
                low(u)

            def gate_round(r):
                with pool.Fori(0, EP) as i:
                    g = pool.snap(i + r * EP)
                    for j in range(2):
                        c = slice(j * NB, (j + 1) * NB)
                        pool.wait_ge(sig_ready, g * 2 + (j + 1))
                        pool.wait_ge(act_ready, g * 2 + 1)
                        pl.tensor_tensor(gated[:, c], glu[:, c], sig[:, c], ALU.mult) \
                          .then_inc(gated_ready, 1)

            gate_round(0)
            further_rounds(pool, gate_round)

            pool.wait_ge(final_in, 16)
            pool.wait_ge(summed_up, 1)
            for h in range(2):
                cols = slice(h * NB, (h + 1) * NB)
                pl.tensor_tensor(xn2[:, 0, cols], xs[:, 0, cols], fnb[:, cols], ALU.mult).then_inc(scaled, 1)

        @block.tensor
        def _(pe):
            mm, tr = nc.tensor.matmul, nc.tensor.transpose

            def split(u):
                pe.wait_ge(low_odd if u % 2 else low_even, u // 2 + 1)

            def mm3(out_, stationary, moving, start, stop):
                mm(out_, stationary[0], moving[0], start=start, stop=False)
                mm(out_, stationary[0], moving[1], start=False, stop=False)
                return mm(out_, stationary[1], moving[0], start=False, stop=stop)

            xn_parts = (xnH, xnL)

            pe.wait_ge(ident_ready, 1)
            pe.wait_ge(pv_in, 16 * 7)
            tr(bank[5][:, 0:PV_ROWS], pv[:, :], ident[0:PV_ROWS, 0:PV_ROWS]).then_inc(pv_full, 1)

            def transposed(n0, src):
                for n in range(4):
                    b, before_ = use(n0 + n)
                    if before_:
                        pe.wait_ge(free[b], before_)
                    for c in range(2):
                        for t in range(TT):
                            last = tr(bank[b][:, (c * TT + t) * P:(c * TT + t + 1) * P],
                                      src[:, t, (2 * n + c) * P:(2 * n + c + 1) * P], ident[:])
                    last.then_inc(full[b], 1)

            pe.wait_ge(xn_ready, TT)
            transposed(U_XNT, xn)

            for n in range(4):
                pe.wait_ge(free[n], 1)
            pe.wait_ge(wf_in, 16)
            for k in range(DC):
                last = mm(bank[4][0:HEADS, 0:T], wf[:, k, :], xnT[:, k, :], start=(k == 0), stop=(k == DC - 1))
            last.then_inc(f_full, 1)

            def columns(n0, n, ch0, src, part=(0, 1)):
                b, before_ = use(n0 + n)
                ch = ch0 + n // 2
                if 0 in part:
                    split(2 * ch0 + n)
                    pe.wait_ge(free[b], before_)
                for c in part:
                    col = (2 * (n % 2) + c) * P
                    for k in range(DC):
                        last = mm3(bank[b][:, c * T:(c + 1) * T],
                                   (w_high(ch)[:, k, col:col + P], w_low(ch)[:, k, col:col + P]),
                                   (src[0][:, k, :], src[1][:, k, :]), start=(k == 0), stop=(k == DC - 1))
                if 1 in part:
                    last.then_inc(full[b], 1)

            def token_rows(b, src, t, ch, ready=None):
                for k in range(DC):
                    if ready is not None and k % 2 == 0:
                        pe.wait_ge(ready, k // 2 + 1)
                    last = mm3(b[:, :], (src[0][:, k, t * P:(t + 1) * P], src[1][:, k, t * P:(t + 1) * P]),
                               (w_high(ch)[:, k, :], w_low(ch)[:, k, :]), start=(k == 0), stop=(k == DC - 1))
                return last

            def gates(c):
                pe.wait_ge(xc_ready, c + 1)
                if c >= 2:
                    pe.wait_ge(gates_read, c - 1)
                for g in range(2):
                    last = mm(bank[6 + c % 2][:, g * T:(g + 1) * T], wbd[:, g, c, :], xc[:, c, :],
                              start=True, stop=True)
                last.then_inc(gates_full, 1)

            pe.wait_ge(xnL_ready, 4)
            for n in range(4):
                columns(U_X, n, CH_X, xn_parts)
            pe.wait_ge(wbd_in, 16 * 4)
            for n in range(4):
                columns(U_Q, n, CH_Q, xn_parts)
                if n:
                    gates(n - 1)
            for n in range(4):
                columns(U_K, n, CH_K, xn_parts)
                gates(n + 3)
            for n in range(4):
                half, t = n // 2, n % 2
                b, before_ = use(U_V + n)
                for h in range(2):
                    split(2 * (CH_V + half) + h)
                pe.wait_ge(free[b], before_)
                last = token_rows(bank[b], xn_parts, t, CH_V + half)
                last.then_inc(full[b], 1)
                if n == 0:
                    gates(DC - 1)

            def scores(p):
                if p == 0:
                    pe.wait_ge(negc_ready, 1)
                    for n in range(4):
                        pe.wait_ge(free[use(U_K + n)[0]], use(U_K + n)[1] + 1)
                else:
                    pe.wait_ge(scores_read, 2 * p)
                for a in range(2):
                    h = 2 * p + a
                    mm(bank[4 + a][:, 0:3 * P], head_rows[:, h:h + 1].to_broadcast([P, P]), negc_parts[:, :],
                       start=True, stop=False)
                for t in (1, 0):
                    for a in range(2):
                        rows = slice(DH * a, DH * (a + 1))
                        last = mm(bank[4 + a][:, t * P:t * P + (t + 1) * P], qT[rows, p, t * P:(t + 1) * P],
                                  kT[rows, p, 0:(t + 1) * P], start=False, stop=(t == 0))
                        if t == 0:
                            last.then_inc(scores_full, 1)

            def probs_transposed(p, a):
                pe.wait_ge(probs_ready, 2 * p + a + 1)
                if p or a:
                    pe.wait_ge(pt_read, 2 * p + a)
                for j in range(3):
                    last = tr(bank[6][:, j * P:(j + 1) * P], probs[:, p % 2, a, j * P:(j + 1) * P], ident[:])
                last.then_inc(pt_full, 1)

            def values(p, a):
                h = 2 * p + a
                rows = slice(DH * a, DH * (a + 1))
                pe.wait_ge(pt_read, 2 * p + a + 1)
                if p and a == 0:
                    pe.wait_ge(attn_ready, p)
                mm(bank[7][rows, 0:T], vS[:, 0, h * DH:(h + 1) * DH], pT[:, a, 0:T], start=True, stop=False)
                last = mm(bank[7][rows, P:T], vS[:, 1, h * DH:(h + 1) * DH], pT[:, a, T:3 * P],
                          start=False, stop=True)
                if a == 1:
                    last.then_inc(o_full, 1)

            for s in range(STEPS):
                p = s - 1
                if s < PAIRS:
                    if s == 0:
                        pe.wait_ge(gates_read, DC)
                    scores(s)
                if 0 <= p < PAIRS:
                    if p == 0:
                        for m in range(4):
                            pe.wait_ge(free[use(U_V + m)[0]], use(U_V + m)[1] + 1)
                    probs_transposed(p, 0)
                columns(U_Y, s, CH_Y, xn_parts, part=(0,))
                if 0 <= p < PAIRS:
                    values(p, 0)
                    probs_transposed(p, 1)
                columns(U_Y, s, CH_Y, xn_parts, part=(1,))
                if 0 <= p < PAIRS:
                    values(p, 1)

            pe.wait_ge(attn_ready, PAIRS)
            for n in range(4):
                columns(U_AP, n, CH_AP, (attnH, attnL))
            pe.wait_ge(recL_ready, 4)
            for n in range(4):
                columns(U_RP, n, CH_RP, (recH, recL))
            def transposed2(t):
                for h in range(2):
                    b, before_ = use(U_XNT2 + 2 * t + h)
                    pe.wait_ge(free[b], before_)
                    pe.wait_ge(xn_ready, TT + 2 * t + h + 1)
                    for c in range(4):
                        last = tr(bank[b][:, c * P:(c + 1) * P], xn2[:, t, (4 * h + c) * P:(4 * h + c + 1) * P],
                                  ident[:])
                    last.then_inc(full[b], 1)

            def logits(t):
                for k in range(DC):
                    if k % 4 == 0:
                        b, before_ = use(U_XNT2 + 2 * t + k // 4)
                        pe.wait_ge(free[b], before_ + 1)
                    last = mm(bank[4 + 2 * t][:, 0:E], xn2T[:, k, t * P:(t + 1) * P], rw[:, k, :],
                              start=(k == 0), stop=(k == DC - 1))
                last.then_inc(logits_full, 1)

            for n in range(4):
                t, half = n // 2, n % 2
                b, before_ = use(U_O + n)
                if n == 3:
                    transposed2(0)
                for h in range(2):
                    split(2 * (CH_O + half) + h)
                pe.wait_ge(free[b], before_)
                last = token_rows(bank[b], (mergedH, mergedL), t, CH_O + half, merged_ready)
                last.then_inc(full[b], 1)

            def row_on_slots(out_, rows, n):
                p0 = 32 if rows is b2s else 0
                k = 4 if rows is b2s else 8
                return mm(out_, ident[p0:p0 + k, p0 + n:p0 + n + 1].to_broadcast([k, CAP]), rows[:, :],
                          start=True, stop=False)

            def first_biases(banks):
                for b in banks:
                    for e in range(2):
                        last = row_on_slots(H[b][e * CAP:(e + 1) * CAP, :], b1s, e * 4 + b)
                return last

            pe.wait_ge(rw_in, 16)
            logits(0)
            pe.wait_ge(b1_full, 16)
            first_biases((0, 1))
            transposed2(1)
            logits(1)
            first_biases((2, 3)).then_inc(b1_used, 1)
            pe.wait_ge(consts_ready, 6)
            pe.wait_ge(mask_ready, 1)
            mm(bank[7][:, 0:E], before[:], mask[:, 0, :], start=True, stop=True)
            mm(bank[7][:, E:2 * E], ones[:], mask[:, 0, :], start=True, stop=False)
            pe.wait_ge(mask_ready, 2)
            mm(bank[7][:, E:2 * E], before[:], mask[:, 1, :], start=False, stop=True)
            mm(bank[7][:, 2 * E:3 * E], ones[:], mask[:, 0, :], start=True, stop=False)
            mm(bank[7][:, 2 * E:3 * E], ones[:], mask[:, 1, :], start=False, stop=True).then_inc(pos_full, 1)

            def gather(number):
                pe.wait_ge(sel_ready, number)
                for j in range(2):
                    for c in range(4):
                        for t in range(TT):
                            last = mm(G[j][:, c * P:(c + 1) * P],
                                      xn2[:, t, (4 * j + c) * P:(4 * j + c + 1) * P], sel[:, t, :],
                                      start=(t == 0), stop=(t == TT - 1))
                    last.then_inc(g_full[j], 1)

            def scatter(uses, y_out, last=False):
                for n in range(4):
                    t, half = n // 2, n % 2
                    if t == 0:
                        pe.wait_ge((y0_out, y1_out)[half], y_out)
                    if t == 0 or not last:
                        pe.wait_ge(g_free[half], uses[half] + t)
                    mm((Y if last and t else G)[half][:, :], selGT[:, t, :], yS[:, half * NB:(half + 1) * NB],
                       start=True, stop=True).then_inc(g_full[half], 1)

            def expert_round(r):
                u0, u1 = r * G0_ROUND, r * G1_ROUND
                if not isinstance(r, int):
                    pe.wait_ge(g_free[0], u0)
                    pe.wait_ge(g_free[1], u1)
                gather(r * (EP + 1) + 1)
                def pair(i, odd):
                    g = pe.snap(i + r * EP)
                    a0 = u0 + 1 + i * G0_PAIR
                    a1 = u1 + 1 + i * G1_PAIR
                    pe.wait_ge(g_free[0], a0)
                    pe.wait_ge(g_free[1], a1)
                    for k in range(W1_CHUNKS):
                        s_ = SLOT_OF[odd * PAIR_CHUNKS + k]
                        w = expert_slot(odd, k).rearrange("p (e n) -> p e n", e=2)
                        pe.wait_ge(slot_full[s_], slot_fill(g, odd, k))
                        for b in range(4):
                            for e in range(2):
                                s = slice(e * CAP, (e + 1) * CAP)
                                last = mm(H[b][s, :], xgT[:, k, s], w[:, e, b * NB:(b + 1) * NB],
                                          start=False, stop=(k == W1_CHUNKS - 1))
                            if k == W1_CHUNKS - 1:
                                last.then_inc(hidden_full, 1)
                        if k < W1_CHUNKS - 1:
                            last.then_inc(w1_used, 1)
                        if k == 1:
                            pe.wait_ge(scatter_empty, r + 1)
                            scatter((a0, a1), g + 1)
                        if k == 2:
                            pe.wait_ge(selG_ready, g + 1)
                            pe.wait_ge(g_free[0], a0 + 2)
                            for t in range(TT):
                                last = tr(G[0][:, t * P:(t + 1) * P], selG[:, t, :], ident[:])
                            last.then_inc(g_full[0], 1)
                        if k == 3:
                            pe.wait_ge(b2_full, g * 16 + 16)
                            for half in range(2):
                                for e in range(2):
                                    row_on_slots(Y[half][e * CAP:(e + 1) * CAP, :], b2s, e * 2 + half)
                        if k == 4:
                            pe.wait_ge(g_free[0], a0 + 3)
                            pe.wait_ge(g_free[1], a1 + 2)
                            gather(r * (EP + 1) + (i + 2))
                    for j in range(2):
                        pe.wait_ge(act_ready, g * 2 + (j + 2))
                        if j == 0:
                            pe.wait_ge(g_free[1], a1 + 3)
                        else:
                            pe.wait_ge(g_free[0], a0 + 4)
                        for c in range(4):
                            last = tr(G[1 - j][:, c * P:(c + 1) * P],
                                      actS[:, (4 * j + c) * P:(4 * j + c + 1) * P], ident[:])
                        last.then_inc(g_full[1 - j], 1)
                    pe.wait_ge(g_free[1], a1 + 4)
                    for m in range(W2_CHUNKS):
                        s_ = SLOT_OF[odd * PAIR_CHUNKS + W1_CHUNKS + m]
                        w = expert_slot(odd, W1_CHUNKS + m).rearrange("p (e k n) -> p e k n", e=2, k=2)
                        pe.wait_ge(slot_full[s_], slot_fill(g, odd, W1_CHUNKS + m))
                        if m == 2:
                            pe.wait_ge(g_free[0], a0 + 5)
                        for kk in range(2):
                            k = 2 * m + kk
                            for half in range(2):
                                for e in range(2):
                                    s = slice(e * CAP, (e + 1) * CAP)
                                    last = mm(Y[half][s, :], actT[:, k, s], w[:, e, kk, half * NB:(half + 1) * NB],
                                              start=False, stop=(k == DC - 1))
                                if k == DC - 1:
                                    last.then_inc(y_full, 1)
                        if m < W2_CHUNKS - 1:
                            last.then_inc(w2_used, 1)
                        if m == 0:
                            pe.wait_ge(glu_ready, g * 2 + 3)
                            pe.wait_ge(b1_full, g * 16 + 32)
                            first_biases((0, 1))
                        if m == 1:
                            pe.wait_ge(lin_ready, g * 2 + 3)
                            first_biases((2, 3)).then_inc(b1_used, 1)

                with pe.Fori(0, EP // 2) as ii:
                    for odd in range(2):
                        pair(pe.snap(ii * 2 + odd), odd)
                done = (r + 1) * EP
                scatter((u0 + 1 + EP * G0_PAIR, u1 + 1 + EP * G1_PAIR), done + 1, last=True)

            def slot_fill(g, odd, j):
                def incs(ns):
                    return sum(16 if n % PAIR_CHUNKS < W1_CHUNKS else 32 for n in ns if SLOT_OF[n] == s)

                s = SLOT_OF[odd * PAIR_CHUNKS + j]
                mix = 16 * len([n for n in range(MIX_CHUNKS) if n % RAW == s])
                upto = incs(range(odd * PAIR_CHUNKS + j + 1))
                assert incs(range(TWO)) % 2 == 0
                return (g - odd) * (incs(range(TWO)) // 2) + (mix + upto)

            expert_round(0)
            further_rounds(pe, expert_round)

        @block.scalar
        def _(act):
            step = [0]
            fn = nc.scalar.activation

            def link(ins):
                step[0] += 1
                ins.then_inc(act_step, 1)
                act.wait_ge(act_step, step[0])

            def root(k, t):
                act.wait_ge(ms_ready, TT * k + t + 1)
                fn(stat[:, TT + t:TT + t + 1], stat[:, t:t + 1], ACT.Sqrt, bias=eps[:, 0:1]).then_inc(std_ready, 1)

            act.wait_ge(eps_ready, 1)
            for t in range(TT):
                root(0, t)
            act.wait_ge(pvT_ready, 1)
            link(fn(sp[:, 0, :], pvT[:, PV_LAM:PV_LAM + DC], ACT.Abs))
            link(fn(sp[:, 0, :], sp[:, 0, :], ACT.Exp, scale=-1.0))
            fn(sp[:, 0, :], sp[:, 0, :], ACT.Ln, bias=1.0).then_inc(lam_l, 1)
            for n in (0, 2):
                b, before_ = use(U_XNT + n)
                act.wait_ge(full[b], before_ + 1)
                for c in range(2):
                    last = fn(xnT[:, 2 * n + c, :], bank[b][:, c * T:(c + 1) * T], ACT.Copy,
                              scale=pvT[:, PV_N1 + 2 * n + c:PV_N1 + 2 * n + c + 1])
                last.then_inc(free[b], 1)
            for n in range(4):
                act.wait_ge(free[n], 1)
                c = slice(2 * n, 2 * n + 2)
                fn(xnH[:, c, :], xnT[:, c, :], ACT.Copy).then_inc(xnH_ready, 1)

            def split_high(u):
                if u >= HALF_CHUNKS:
                    return
                n, c = u // 2, half_cols(u)
                act.wait_ge(slot_full[n % RAW], 16 * (n // RAW + 1))
                if n >= 2:
                    wait_mix_half_used(act, n - 2, u % 2)
                fn(w_high(n)[:, :, c], chunk(n)[:, :, c], ACT.Copy).then_inc(high, 1)

            for u in range(4):
                split_high(u)
            act.wait_ge(f_full, 1)
            act.wait_ge(fb_in, 16)
            link(fn(ftmp[:, 0:T], bank[4][0:HEADS, 0:T], ACT.Abs, bias=fb[:, 0:1]))
            link(fn(ftmp[:, 0:T], ftmp[:, 0:T], ACT.Exp, scale=-1.0))
            fn(ftmp[:, 0:T], ftmp[:, 0:T], ACT.Ln, bias=1.0).then_inc(f_l, 1)

            act.wait_ge(xp_zero, 1)

            def out_of_bank(n, dst, **how):
                b, before_ = use(n)
                act.wait_ge(full[b], before_ + 1)
                fn(dst, bank[b][:, :].rearrange("p (c t) -> p c t", c=2), ACT.Copy, **how).then_inc(free[b], 1)

            for n in range(4):
                out_of_bank(U_X + n, xp[:, 2 * n:2 * n + 2, CONV - 1:])
                split_high(2 * CH_X + n + 4)

            def gates(c):
                act.wait_ge(gates_full, c + 1)
                if c == 0:
                    act.wait_ge(sp_ready, 1)
                z = bank[6 + c % 2]
                link(fn(aT[:, c, :], z[:, 0:T], ACT.Tanh, bias=pvH[:, PV_BA + c:PV_BA + c + 1], scale=0.5))
                fn(ixT[:, c, :], z[:, T:2 * T], ACT.Tanh, bias=pvH[:, PV_BX + c:PV_BX + c + 1],
                   scale=0.5).then_inc(gates_read, 1)
                link(fn(uT[:, c, :], aT[:, c, :], ACT.Tanh, bias=sp[:, 1, c:c + 1], scale=sp[:, 1, c:c + 1]))
                fn(aT[:, c, :], aT[:, c, :], ACT.Exp, bias=sp[:, 2, c:c + 1],
                   scale=sp[:, 2, c:c + 1]).then_inc(lru_u, 1)

            for n in range(4):
                out_of_bank(U_Q + n, qT[:, 2 * n:2 * n + 2, :], scale=DH ** -0.5)
                split_high(2 * CH_Q + n + 4)
                if n:
                    gates(n - 1)
            for n in range(4):
                gates(n + 3)
                split_high(2 * CH_K + n + 4)
            for n in range(4):
                half, t = n // 2, n % 2
                b, before_ = use(U_V + n)
                act.wait_ge(full[b], before_ + 1)
                fn(vS[:, t, half * NB:(half + 1) * NB], bank[b][:, :], ACT.Copy).then_inc(free[b], 1)
                if n == 0:
                    gates(DC - 1)
                if t == 1:
                    for h in range(2):
                        split_high(2 * (CH_V + half) + h + 4)
                if n == 1:
                    act.wait_ge(lru_m, DC)
                    fn(uT, uT, ACT.Sqrt, scale=0.5).then_inc(lru_root, 1)

            def pt_out(p, a):
                act.wait_ge(pt_full, 2 * p + a + 1)
                if p:
                    act.wait_ge(o_full, p)
                fn(pT[:, a, :], bank[6][:, 0:3 * P], ACT.Copy).then_inc(pt_read, 1)

            for s in range(STEPS):
                p = s - 1
                if 0 <= p < PAIRS:
                    pt_out(p, 0)
                if s < PAIRS:
                    for a in range(2):
                        act.wait_ge(negmx_ready, 2 * s + a + 1)
                        for t in range(2):
                            cols = slice(t * P, t * P + (t + 1) * P)
                            m = 2 * a + t
                            last = fn(probs[:, s % 2, a, cols], probs[:, s % 2, a, cols], ACT.Exp,
                                      bias=mx[:, s % 2, m:m + 1], accum_out=den[:, s % 2, m:m + 1])
                            last.then_inc(exp_ready, 1)
                if s:
                    split_high(2 * CH_Y + s + 3)
                if 0 <= p < PAIRS:
                    pt_out(p, 1)
                if s == 0:
                    act.wait_ge(gates_full, DC)
                if s in Y_STEPS:
                    n = Y_STEPS.index(s)
                    out_of_bank(U_Y + s, yT[:, 2 * n:2 * n + 2, :])
                else:
                    n = G_STEPS.index(s)
                    b, before_ = use(U_Y + s)
                    act.wait_ge(full[b], before_ + 1)
                    if n == 0:
                        act.wait_ge(xc_ready, DC)
                    for c in range(2):
                        k = 2 * n + c
                        last = fn((gA if k < DC else gR)[:, k % DC, :], bank[b][:, c * T:(c + 1) * T], ACT.Tanh,
                                  bias=pvH[:, PV_GB + k:PV_GB + k + 1], scale=0.5)
                    last.then_inc(free[b], 1)
                if 0 <= p < PAIRS:
                    act.wait_ge(o_full, p + 1)
                    fn(attnH[:, p, :], bank[7][:, 0:T], ACT.Copy).then_inc(o_read, 1)
                if s - 1 in Y_STEPS:
                    n = Y_STEPS.index(s - 1)
                    c = slice(2 * n, 2 * n + 2)
                    act.wait_ge(gelu_arg, n + 1)
                    fn(gtmp[:, c, :], gtmp[:, c, :], ACT.Tanh, scale=GELU_C).then_inc(gelu_tanh, 1)
                    act.wait_ge(rec_ready, n + 1)
                    fn(recH[:, c, :], hT[:, c, :], ACT.Copy).then_inc(recH_ready, 1)
            split_high(2 * CH_Y + STEPS + 3)

            for n in range(4):
                split_high(2 * CH_AP + n + 4)
            wait_mix_chunk_used(act, CH_AP + 1)
            act.dma_start(rw, router_w[0].rearrange("(k p) e -> p k e", p=P)).then_inc(rw_in, 16)
            act.dma_start(rb[:], router_b[0].partition_broadcast(P)).then_inc(rb_in, 16)
            act.dma_start(n2b, norm2_scale[0].partition_broadcast(P)).then_inc(norms_in, 16)

            for n in range(4):
                c = slice(2 * n, 2 * n + 2)
                split_high(2 * CH_RP + n + 4)
                act.wait_ge(summed, n + 1)
                fn(mergedH[:, c, :], gA[:, c, :], ACT.Copy).then_inc(mergedH_ready, 1)

            def xn2T_out(t):
                b, before_ = use(U_XNT2 + 2 * t)
                act.wait_ge(full[b], before_ + 1)
                fn(xn2T[:, 0:4, t * P:(t + 1) * P], bank[b][:, :].rearrange("p (c t) -> p c t", c=4),
                   ACT.Copy).then_inc(free[b], 1)

            root(1, 0)
            xn2T_out(0)
            root(1, 1)
            xn2T_out(1)
            act.wait_ge(xn_ready, TT + 4)
            act.dma_start(fnb, final_norm_scale.partition_broadcast(P)).then_inc(final_in, 16)
            for t in range(TT):
                act.wait_ge(top_neg, t + 1)
                fn(gk[:, t, :], top8[:, t, 0:TOPK], ACT.Exp, bias=rout[:, t:t + 1],
                   accum_out=rout[:, 2 + t:3 + t]).then_inc(top_exp, 1)

            def gather_out(uses):
                for j in range(2):
                    act.wait_ge(g_full[j], uses[j] + 1)
                    fn(xgT[:, 4 * j:4 * j + 4, :], G[j][:, :].rearrange("p (c s) -> p c s", c=4),
                       ACT.Copy).then_inc(g_free[j], 1)

            def expert_round(r):
                u0, u1 = r * G0_ROUND, r * G1_ROUND
                gather_out((u0, u1))
                with act.Fori(0, EP) as i:
                    g = act.snap(i + r * EP)
                    a0 = u0 + 1 + i * G0_PAIR
                    a1 = u1 + 1 + i * G1_PAIR
                    act.wait_ge(g_full[0], a0 + 3)
                    fn(selGT, G[0][:, 0:2 * P].rearrange("p (t s) -> p t s", t=TT), ACT.Copy).then_inc(g_free[0], 1)
                    for j in range(2):
                        c = slice(j * NB, (j + 1) * NB)
                        act.wait_ge(glu_ready, g * 2 + (j + 2))
                        act.wait_ge(gated_ready, g * 2 + 1)
                        fn(sig[:, c], glu[:, c], ACT.Sigmoid, scale=ALPHA).then_inc(sig_ready, 1)
                    act.wait_ge(hidden_full, g * 4 + 4)
                    gather_out((a0 + 3, a1 + 2))
                    for j in range(2):
                        act.wait_ge(g_full[1 - j], (a1 + 4) if j == 0 else (a0 + 5))
                        fn(actT[:, 4 * j:4 * j + 4, :], G[1 - j][:, :].rearrange("p (c s) -> p c s", c=4),
                           ACT.Copy).then_inc(g_free[1 - j], 1)
                    act.wait_ge(y_full, g * 2 + 1)
                    fn(yS[:, 0:NB], Y[0][:, :], ACT.Copy).then_inc(y0_out, 1)

            expert_round(0)
            further_rounds(act, expert_round)

            for t in range(TT):
                root(2, t)
            for h in range(2):
                cols = slice(h * NB, (h + 1) * NB)
                act.wait_ge(scaled, h + 1)
                act.wait_ge(inv_ready, 1)
                fn(xn2[:, 0, cols], xn2[:, 0, cols], ACT.Copy, scale=stat[:, 2 * TT:2 * TT + 1]).then_inc(fin_ready[0], 1)

        @block.vector
        def _(dve):
            step = [0]
            v = nc.vector

            def link(ins):
                step[0] += 1
                ins.then_inc(dve_step, 1)
                dve.wait_ge(dve_step, step[0])

            def half(n):
                return slice(n * NB, (n + 1) * NB)

            def square_sum(t, h):
                link(v.tensor_tensor_reduce(out=squares[:, t, half(h)], in0=xs[:, t, half(h)], in1=xs[:, t, half(h)],
                                            scale=1.0, scalar=0.0, op0=ALU.mult, op1=ALU.add,
                                            accum_out=sumsq[:, t, h:h + 1]))

            def mean_square(t):
                v.tensor_scalar(stat[:, t:t + 1], sumsq[:, t, 0:1], sumsq[:, t, 1:2], 1.0 / D,
                                ALU.add, ALU.mult).then_inc(ms_ready, 1)

            def inv_rms(k, t):
                dve.wait_ge(std_ready, TT * k + t + 1)
                link(v.reciprocal(stat[:, 2 * TT + t:2 * TT + t + 1], stat[:, TT + t:TT + t + 1]))
                return stat[:, 2 * TT + t:2 * TT + t + 1]

            for t in range(TT):
                dve.wait_ge(x_in[t], 16)
                for h in range(2):
                    square_sum(t, h)
                mean_square(t)
            for t in range(TT):
                v.tensor_scalar(xn[:, t, :], xs[:, t, :], inv_rms(0, t), None, ALU.mult).then_inc(xn_ready, 1)
            dve.wait_ge(pv_full, 1)
            v.tensor_copy(pvT[:], bank[5][:, 0:PV_ROWS]).then_inc(pvT_ready, 1)
            dve.wait_ge(pvT_ready, 1)
            link(v.tensor_scalar(pvH[:], pvT[:], 0.5, None, ALU.mult))
            link(v.tensor_scalar(sp[:, 1, :], pvT[:, PV_LAM:PV_LAM + DC], -1.0, 0.0, ALU.mult, ALU.max))
            dve.wait_ge(lam_l, 1)
            link(v.tensor_tensor(sp[:, 1, :], sp[:, 1, :], sp[:, 0, :], ALU.add))
            link(v.tensor_scalar(sp[:, 1, :], sp[:, 1, :], LRU_C / 2, None, ALU.mult))
            v.tensor_scalar(sp[:, 2, :], sp[:, 1, :], -1.0, None, ALU.mult).then_inc(sp_ready, 1)
            for n in (1, 3):
                b, before_ = use(U_XNT + n)
                dve.wait_ge(full[b], before_ + 1)
                for c in range(2):
                    last = v.tensor_scalar(xnT[:, 2 * n + c, :], bank[b][:, c * T:(c + 1) * T],
                                           pvT[:, PV_N1 + 2 * n + c:PV_N1 + 2 * n + c + 1], None, ALU.mult)
                last.then_inc(free[b], 1)
            for n in range(4):
                dve.wait_ge(xnH_ready, n + 1)
                c = slice(2 * n, 2 * n + 2)
                v.tensor_tensor(xnL[:, c, :], xnT[:, c, :], xnH[:, c, :], ALU.subtract).then_inc(xnL_ready, 1)

            def low(u):
                if u % 2 == 0 and u < HALF_CHUNKS:
                    split_low(dve, v, u, low_even)

            low(0)
            low(2)
            dve.wait_ge(f_l, 1)
            link(v.tensor_scalar(ftmp[:, T:2 * T], bank[4][0:HEADS, 0:T], fb[:, 0:1], 0.0, ALU.add, ALU.min))
            link(v.tensor_tensor(ftmp[:, 0:T], ftmp[:, 0:T], ftmp[:, T:2 * T], ALU.subtract))
            link(v.memset(ftmp[:, T:2 * T], 1.0))
            link(v.tensor_tensor_scan(negc[:, P:P + T], ftmp[:, T:2 * T], ftmp[:, 0:T], 0.0, ALU.mult, ALU.add))
            link(v.tensor_copy(negc[:, 0:P], negc[:, P:2 * P]))
            dve.wait_ge(rows_zero, 2)
            dve.wait_ge(ident_ready, 1)
            link(v.tensor_copy(negc_parts[0:HEADS, :], negc))
            link(v.tensor_tensor(negc, negc, negc_parts[0:HEADS, :], ALU.subtract))
            link(v.tensor_copy(negc_parts[32:32 + HEADS, :], negc))
            link(v.tensor_copy(head_rows[0:HEADS, :], ident[0:HEADS, 0:HEADS]))
            v.tensor_copy(head_rows[32:32 + HEADS, :], ident[32:32 + HEADS, 32:32 + HEADS]).then_inc(negc_ready, 1)

            def conv(c):
                w = [pvT[:, PV_CW + j * DC + c:PV_CW + j * DC + c + 1] for j in range(CONV)]
                link(v.tensor_scalar(xc[:, c, :], xp[:, c, 0:T], w[0], pvT[:, PV_CB + c:PV_CB + c + 1],
                                     ALU.mult, ALU.add))
                for j in range(1, CONV):
                    ins = v.scalar_tensor_tensor(xc[:, c, :], xp[:, c, j:j + T], w[j], xc[:, c, :], ALU.mult, ALU.add)
                    if j < CONV - 1:
                        link(ins)
                    else:
                        ins.then_inc(xc_ready, 1)

            def lru_gates(c):
                dve.wait_ge(lru_u, c + 1)
                v.scalar_tensor_tensor(ixT[:, c, :], ixT[:, c, :], 1.0, xc[:, c, :], ALU.add, ALU.mult) \
                 .then_inc(lru_i, 1)
                dve.wait_ge(lru_i, c + 1)
                link(v.tensor_scalar(xc[:, c, :], uT[:, c, :], 1.0, None, ALU.add))
                link(v.reciprocal(xc[:, c, :], xc[:, c, :]))
                v.scalar_tensor_tensor(uT[:, c, :], uT[:, c, :], 1e-30, xc[:, c, :], ALU.max, ALU.mult) \
                 .then_inc(lru_m, 1)

            def k_out(n):
                b, before_ = use(U_K + n)
                dve.wait_ge(full[b], before_ + 1)
                v.tensor_copy(kT[:, 2 * n:2 * n + 2, :], bank[b][:, :].rearrange("p (c t) -> p c t", c=2)) \
                 .then_inc(free[b], 1)

            for c in range(DC):
                if c % 2 == 0:
                    b, before_ = use(U_X + c // 2)
                    dve.wait_ge(free[b], before_ + 1)
                conv(c)
                if c % 2 == 1:
                    low(2 * CH_X + c // 2 + 4)
            low(2 * CH_Q + 4)
            for c in range(3):
                lru_gates(c)
                low(2 * CH_Q + c + 5)
            for n in range(4):
                k_out(n)
                lru_gates(n + 3)
                low(2 * CH_K + n + 4)
            lru_gates(DC - 1)
            low(2 * CH_V + 4)
            dve.wait_ge(lru_root, 1)
            link(v.memset(uT[:, :, 0:1], 0.5))
            link(v.tensor_tensor(row(5), row(4), row(5), ALU.mult))
            for c in range(DC):
                v.tensor_tensor_scan(hT[:, c, :], aT[:, c, :], ixT[:, c, :], 0.0, ALU.mult, ALU.add).then_inc(h_ready, 1)
            low(2 * CH_V + 6)

            def softmax(p):
                q = p % 2
                if p == 0:
                    dve.wait_ge(consts_ready, 6)
                for a in range(2):
                    dve.wait_ge(scores_full, 2 * p + a + 1)
                    if p >= 2:
                        dve.wait_ge(pt_full, 2 * (p - 2) + a + 1)
                    for t in range(2):
                        cols = slice(t * P, t * P + (t + 1) * P)
                        m = 2 * a + t
                        last = v.tensor_tensor_reduce(
                            out=probs[:, q, a, cols], in0=bank[4 + a][:, cols],
                            in1=causal[:, :, :].rearrange("p a b -> p (a b)")[:, cols], scale=1.0,
                            scalar=NEG, op0=ALU.add, op1=ALU.max, accum_out=mx[:, q, m:m + 1])
                    last.then_inc(scores_read, 1)
                    dve.wait_ge(scores_read, 2 * p + a + 1)
                    v.tensor_scalar(mx[:, q, 2 * a:2 * a + 2], mx[:, q, 2 * a:2 * a + 2], -1.0, None,
                                    ALU.mult).then_inc(negmx_ready, 1)
                if p:
                    low(2 * CH_Y + p + 3)
                for a in range(2):
                    dve.wait_ge(exp_ready, 4 * p + 2 * a + 2)
                    link(v.reciprocal(den[:, q, 2 * a:2 * a + 2], den[:, q, 2 * a:2 * a + 2]))
                    for t in range(2):
                        cols = slice(t * P, t * P + (t + 1) * P)
                        m = 2 * a + t
                        last = v.tensor_scalar(probs[:, q, a, cols], probs[:, q, a, cols],
                                               den[:, q, m:m + 1], None, ALU.mult)
                    last.then_inc(probs_ready, 1)

            def gelu_in(n):
                c = slice(2 * n, 2 * n + 2)
                dve.wait_ge(gelu_sq, n + 1)
                v.tensor_scalar(gtmp[:, c, :], gtmp[:, c, :], GELU_A, 1.0, ALU.mult, ALU.add).then_inc(gelu_lin, 1)

            def gelu_out(n):
                c = slice(2 * n, 2 * n + 2)
                dve.wait_ge(gelu_tanh, n + 1)
                link(v.scalar_tensor_tensor(yT[:, c, :], gtmp[:, c, :], 1.0, yT[:, c, :], ALU.add, ALU.mult))
                v.scalar_tensor_tensor(hT[:, c, :], hT[:, c, :], 0.5, yT[:, c, :], ALU.mult, ALU.mult) \
                 .then_inc(rec_ready, 1)

            for s in range(STEPS):
                if s < PAIRS:
                    softmax(s)
                else:
                    low(2 * CH_Y + s + 3)
                if s in Y_STEPS:
                    gelu_in(Y_STEPS.index(s))
                if s - 1 in Y_STEPS:
                    gelu_out(Y_STEPS.index(s - 1))
                if 1 <= s <= PAIRS:
                    dve.wait_ge(o_read, s)
                    v.tensor_tensor(attnL[:, s - 1, :], bank[7][:, 0:T], attnH[:, s - 1, :], ALU.subtract) \
                     .then_inc(attn_ready, 1)
            low(2 * CH_Y + STEPS + 3)

            def gate_product(g_, n0, n):
                c = slice(2 * n, 2 * n + 2)
                b, before_ = use(n0 + n)
                dve.wait_ge(full[b], before_ + 1)
                v.scalar_tensor_tensor(g_[:, c, :], g_[:, c, :], 1.0,
                                       bank[b][:, :].rearrange("p (c t) -> p c t", c=2),
                                       ALU.add, ALU.mult).then_inc(free[b], 1)
                return b, before_

            for n in range(4):
                gate_product(gA, U_AP, n)
                low(2 * CH_AP + n + 4)
            for n in range(4):
                c = slice(2 * n, 2 * n + 2)
                b, before_ = gate_product(gR, U_RP, n)
                dve.wait_ge(free[b], before_ + 1)
                v.tensor_tensor(gA[:, c, :], gA[:, c, :], gR[:, c, :], ALU.add).then_inc(summed, 1)
                if n < 3:
                    low(2 * CH_RP + n + 4)
                dve.wait_ge(mergedH_ready, n + 1)
                v.tensor_tensor(mergedL[:, c, :], gA[:, c, :], mergedH[:, c, :], ALU.subtract).then_inc(merged_ready, 1)
            def x1(t):
                for h in range(2):
                    b, before_ = use(U_O + 2 * t + h)
                    dve.wait_ge(full[b], before_ + 1)
                    v.scalar_tensor_tensor(xs[:, t, half(h)], bank[b][:, :], 0.5, xs[:, t, half(h)],
                                           ALU.mult, ALU.add).then_inc(free[b], 1)
                    dve.wait_ge(free[b], before_ + 1)
                    square_sum(t, h)
                mean_square(t)
                inv = inv_rms(1, t)
                for h in range(2):
                    v.scalar_tensor_tensor(xn2[:, t, half(h)], xs[:, t, half(h)], inv, n2b[:, half(h)],
                                           ALU.mult, ALU.mult).then_inc(xn_ready, 1)

            def xn2T_out(t):
                b, before_ = use(U_XNT2 + 2 * t + 1)
                dve.wait_ge(full[b], before_ + 1)
                v.tensor_copy(xn2T[:, 4:8, t * P:(t + 1) * P], bank[b][:, :].rearrange("p (c t) -> p c t", c=4)) \
                 .then_inc(free[b], 1)

            def choose(t):
                dve.wait_ge(logits_full, t + 1)
                link(v.tensor_tensor(lg[:, t, :], bank[4 + 2 * t][:, 0:E], rb[:, :], ALU.add))
                link(v.max(out=top8[:, t, :], in_=lg[:, t, :]))
                link(v.max_index(out=idx8[:, t, :], in_max=top8[:, t, :], in_values=lg[:, t, :]))
                v.tensor_scalar(rout[:, t:t + 1], top8[:, t, 0:1], -1.0, None, ALU.mult).then_inc(top_neg, 1)
                link(v.tensor_copy(idxf[:, t, :], idx8[:, t, :]))
                link(v.tensor_tensor(oneh[:, t], expert_no[:, :].unsqueeze(1).to_broadcast([P, TOPK, E]),
                                     idxf[:, t, 0:TOPK].unsqueeze(2).to_broadcast([P, TOPK, E]), ALU.is_equal))
                v.tensor_reduce(mask[:, t, :], oneh[:, t].rearrange("p k e -> p e k"), AXX, ALU.add) \
                 .then_inc(mask_ready, 1)

            dve.wait_ge(norms_in, 16)
            dve.wait_ge(rb_in, 16)
            link(v.memset(posm, NOT_HERE))
            x1(0)
            xn2T_out(0)
            x1(1)
            choose(0)
            xn2T_out(1)
            choose(1)
            dve.wait_ge(pos_full, 1)
            link(v.scalar_tensor_tensor(posm[:, :, 0:E], mask, -NOT_HERE,
                                        bank[7][:, 0:TT * E].rearrange("p (t e) -> p t e", t=TT), ALU.mult, ALU.add))
            v.tensor_scalar(posm[:, :, 0:E], posm[:, :, 0:E], NOT_HERE, None, ALU.add).then_inc(posm_ready, 1)

            def gates_and_rounds():
                dve.wait_ge(top_exp, TT)
                link(v.reciprocal(rout[:, 4:6], rout[:, 2:4]))
                link(v.tensor_tensor(gk, gk, rout[:, 4:6].unsqueeze(2).to_broadcast([P, TT, TOPK]), ALU.mult))
                link(v.tensor_tensor(onehG, oneh, gk.unsqueeze(3).to_broadcast([P, TT, TOPK, E]), ALU.mult))
                link(v.tensor_reduce(gateE, onehG.rearrange("p t k e -> p t e k"), AXX, ALU.add))
                link(v.tensor_reduce(rout[:, 6:7], bank[7][:, TT * E:(TT + 1) * E], AXX, ALU.max))
                link(v.tensor_scalar(rout[:, 8:9], rout[:, 6:7], float(CAP), None, ALU.is_gt))
                link(v.tensor_scalar(rout[:, 9:10], rout[:, 6:7], float(2 * CAP), None, ALU.is_gt))
                link(v.tensor_scalar(rout[:, 10:11], rout[:, 6:7], float(3 * CAP), 1.0, ALU.is_gt, ALU.add))
                link(v.tensor_reduce(rout[:, 7:8], rout[:, 8:11], AXX, ALU.add))
                v.tensor_copy(rounds_i[:], rout[:, 7:8]).then_inc(rounds_ready, 1)

            numbers = slot_no[:, :].unsqueeze(1).unsqueeze(1).to_broadcast([P, TT, 2, CAP])
            sel4 = sel.rearrange("p t (e s) -> p t e s", e=2)
            selG4 = selG.rearrange("p t (e s) -> p t e s", e=2)

            def of_pair(table, first):
                return table[:, :, bass.ds(first, 2)].unsqueeze(3).to_broadcast([P, TT, 2, CAP])

            def expert_round(r):
                u0, u1 = r * G0_ROUND, r * G1_ROUND
                if not isinstance(r, int):
                    dve.wait_ge(g_free[0], u0)
                    dve.wait_ge(g_free[1], u1)
                    v.tensor_scalar(posm, posm, -float(CAP), None, ALU.add).then_inc(posm_ready, 1)
                dve.wait_ge(posm_ready, r + 1)
                v.tensor_tensor(sel4, numbers, of_pair(posm, 0), ALU.is_equal).then_inc(sel_ready, 1)
                if isinstance(r, int):
                    link(v.memset(yS, 0.0))
                v.memset(selGT, 0.0).then_inc(scatter_empty, 1)
                if isinstance(r, int):
                    gates_and_rounds()

                def add_back(uses, last=False):
                    for n in range(4):
                        t, half = n // 2, n % 2
                        cols = slice(half * NB, (half + 1) * NB)
                        dve.wait_ge(g_full[half], uses[half] + (t + 1))
                        v.tensor_tensor(xs[:, t, cols], (Y if last and t else G)[half][:, :], xs[:, t, cols],
                                        ALU.add).then_inc(g_free[half], 1)
                    if last:
                        for half in range(2):
                            dve.wait_ge(g_free[half], uses[half] + 2)

                with dve.Fori(0, EP) as i:
                    g = dve.snap(i + r * EP)
                    a0 = u0 + 1 + i * G0_PAIR
                    a1 = u1 + 1 + i * G1_PAIR
                    i2 = i * 2
                    dve.wait_ge(g_full[0], a0)
                    dve.wait_ge(g_full[1], a1)
                    v.tensor_tensor(selG4, numbers, of_pair(posm, i2), ALU.is_equal).then_inc(slots_eq, 1)
                    dve.wait_ge(slots_eq, g + 1)
                    v.tensor_tensor(selG4, selG4, of_pair(gateE, i2), ALU.mult).then_inc(selG_ready, 1)
                    v.tensor_tensor(sel4, numbers, of_pair(posm, i2 + 2), ALU.is_equal).then_inc(sel_ready, 1)
                    add_back((a0, a1))
                    for j in range(2):
                        c = slice(j * NB, (j + 1) * NB)
                        dve.wait_ge(hidden_full, g * 4 + (j + 1))
                        v.tensor_scalar(glu[:, c], H[j][:, :], LIMIT, None, ALU.min).then_inc(glu_ready, 1)
                        dve.wait_ge(hidden_full, g * 4 + (j + 3))
                        v.tensor_scalar(lin[:, c], H[2 + j][:, :], -LIMIT, LIMIT, ALU.max, ALU.min) \
                         .then_inc(lin_ready, 1)
                    for j in range(2):
                        c = slice(j * NB, (j + 1) * NB)
                        dve.wait_ge(gated_ready, g * 2 + (j + 2))
                        dve.wait_ge(lin_ready, g * 2 + (j + 2))
                        v.scalar_tensor_tensor(actS[:, c], lin[:, c], 1.0, gated[:, c], ALU.add, ALU.mult) \
                         .then_inc(act_ready, 1)
                    dve.wait_ge(y_full, g * 2 + 2)
                    v.tensor_copy(yS[:, NB:2 * NB], Y[1][:, :]).then_inc(y1_out, 1)
                add_back((u0 + 1 + EP * G0_PAIR, u1 + 1 + EP * G1_PAIR), last=True)

            expert_round(0)
            further_rounds(dve, expert_round)

            v.memset(mx[:, 0, 0:1], 0.0).then_inc(summed_up, 1)
            for t in range(TT):
                for h in range(2):
                    square_sum(t, h)
                mean_square(t)
            dve.wait_ge(std_ready, TT * 2 + 1)
            v.reciprocal(stat[:, 2 * TT:2 * TT + 1], stat[:, TT:TT + 1]).then_inc(inv_ready, 1)
            inv = inv_rms(2, 1)
            dve.wait_ge(final_in, 16)
            for h in range(2):
                v.scalar_tensor_tensor(xn2[:, 1, half(h)], xs[:, 1, half(h)], inv, fnb[:, half(h)],
                                       ALU.mult, ALU.mult).then_inc(fin_ready[1], 1)


_INS = ["x", "norm1_scale", "w_in", "f_bias", "gate_bias", "conv_w", "conv_b", "rg_wa", "rg_ba", "rg_wx",
        "rg_bx", "rg_lambda", "w_attn_proj", "w_rec_proj", "w_out", "norm2_scale", "router_w", "router_b",
        "moe_w1", "moe_b1", "moe_w2", "moe_b2", "final_norm_scale"]


def kernel(**inputs):
    import numpy as np
    import concourse.bacc as bacc
    from concourse.bass_utils import run_bass_kernel_spmd

    nc = bacc.Bacc("TRN2", target_bir_lowering=False, num_devices=1)
    arrays, args = {}, []
    for name in _INS:
        a = np.ascontiguousarray(inputs[name])
        arrays[f"in_{name}"] = a
        args.append(nc.dram_tensor(f"in_{name}", a.shape, mybir.dt.from_np(a.dtype), kind="ExternalInput").ap())
    args.append(nc.dram_tensor("out_y", (1, T, D), fp32, kind="ExternalOutput").ap())
    build(nc, *args)
    r = run_bass_kernel_spmd(nc, [arrays], core_ids=[0])
    return r.results[0]["out_y"]
```
